# Optimizing a Trainium2 kernel written in Bass

```python
import math
import jax, jax.numpy as jnp
from jax import lax
import numpy as np

'''Hybrid autoregressive decoder trunk, one inference step for two request groups sharing weights.

Each layer: RMSNorm -> one combined input projection whose columns are split between two parallel
head groups (RWKV-7 time mixing, 16 heads x 64; RetNet multi-scale retention, 8 heads x 128) ->
per-group transforms -> concat -> one output projection -> residual add; RMSNorm -> hierarchical MoE
(top-1 of 4 expert groups, then top-2 of 8 SwiGLU experts in that group) -> residual add.
One final RMSNorm.

Inputs:
  x_prompt         (BATCH, SEQ, D_MODEL)          positions 0..SEQ-1, fresh sequences
  x_sample         (DEC_BATCH, DEC_SEQ, D_MODEL)  positions PAST_LEN..PAST_LEN+DEC_SEQ-1
  state_rwkv_shift (DEPTH, DEC_BATCH, RWKV_PROJ)  projected RWKV row of the previous position (token shift)
  state_rwkv_wkv   (DEPTH, DEC_BATCH, A_HEADS, A_HD, A_HD)  RWKV-7 matrix state, (value, key) layout
  state_retention  (DEPTH, DEC_BATCH, R_HEADS, R_HD, R_HD)  retention state, (key, value) layout
  layer weights with leading DEPTH axis; norm_final_g (D_MODEL,)
Returns the tuple:
  y_prompt  (BATCH, SEQ, D_MODEL)
  y_sample  (DEC_BATCH, DEC_SEQ, D_MODEL)
  p_shift   (DEPTH, BATCH, RWKV_PROJ)
  p_wkv     (DEPTH, BATCH, A_HEADS, A_HD, A_HD)
  p_ret     (DEPTH, BATCH, R_HEADS, R_HD, R_HD)
  s_shift   (DEPTH, DEC_BATCH, RWKV_PROJ)
  s_wkv     (DEPTH, DEC_BATCH, A_HEADS, A_HD, A_HD)
  s_ret     (DEPTH, DEC_BATCH, R_HEADS, R_HD, R_HD)
'''

D_MODEL = 2048
BATCH = 1
SEQ = 256
DEPTH = 1
DEC_BATCH = 8
DEC_SEQ = 8
PAST_LEN = 2048
PAGE_SIZE = 128

MIX_W = D_MODEL
A_W = MIX_W // 2
A_HD = 64
A_HEADS = A_W // A_HD
W_LORA = 64
A_LORA = 64
G_LORA = 160
RWKV_PROJ = 3 * A_W + W_LORA + A_LORA + G_LORA
R_W = MIX_W - A_W
R_HEADS = 8
R_HD = R_W // R_HEADS
RET_PROJ = 4 * R_W
PROJ = RWKV_PROJ + RET_PROJ
RET_CHUNK = 128
N_GROUPS = 4
E_PER_GROUP = 8
N_EXPERTS = N_GROUPS * E_PER_GROUP
TOP_K = 2
D_EXPERT = D_MODEL // 4
MOE_BLOCK = 128
NORM_EPS = 1e-6
LNX_EPS = 64e-5
DECAY_SCALE = math.exp(-0.5)

kernel_name = 'hymba_rwkv7_retnet_hmoe_step'

def _rmsnorm(x, g):
    xf = x.astype(jnp.float32)
    y = xf * lax.rsqrt(jnp.mean(xf * xf, axis=-1, keepdims=True) + NORM_EPS)
    return (y * g.astype(jnp.float32)).astype(x.dtype)

def _wkv_step(S, inp):
    r, w, k, v, kk, b = inp
    sa = jnp.einsum('bhvk,bhk->bhv', S, -kk)
    S = S * w[:, :, None, :] + sa[..., :, None] * b[:, :, None, :] + v[..., :, None] * k[:, :, None, :]
    y = jnp.einsum('bhvk,bhk->bhv', S, r)
    return S, y

def _rwkv7(xm, S0, decay_w0, decay_up, iclr_a0, iclr_up, gate_up, k_k, k_a, r_k, lnx_g, lnx_b):
    B, T, _ = xm.shape
    f32 = jnp.float32
    r, k, v, wd, ad, gd = jnp.split(
        xm, [A_W, 2 * A_W, 3 * A_W, 3 * A_W + W_LORA, 3 * A_W + W_LORA + A_LORA], axis=-1)
    w = jnp.exp(-DECAY_SCALE * jax.nn.sigmoid((decay_w0 + jnp.tanh(wd) @ decay_up).astype(f32)))
    a = jax.nn.sigmoid((iclr_a0 + ad @ iclr_up).astype(f32))
    g = jax.nn.sigmoid(gd) @ gate_up
    hd = lambda t: t.astype(f32).reshape(B, T, A_HEADS, A_HD)
    hp = lambda t: t.astype(f32).reshape(A_HEADS, A_HD)
    r, k, v, w, a = hd(r), hd(k), hd(v), hd(w), hd(a)
    kk = k * hp(k_k)
    kk = kk / jnp.maximum(jnp.sqrt(jnp.sum(kk * kk, axis=-1, keepdims=True)), 1e-12)
    k = k * (1.0 + (a - 1.0) * hp(k_a))
    tm = lambda t: jnp.moveaxis(t, 1, 0)
    S_T, y = lax.scan(_wkv_step, S0.astype(f32), (tm(r), tm(w), tm(k), tm(v), tm(kk), tm(kk * a)))
    y = jnp.moveaxis(y, 0, 1)
    mu = jnp.mean(y, axis=-1, keepdims=True)
    var = jnp.mean(jnp.square(y - mu), axis=-1, keepdims=True)
    y = (y - mu) * lax.rsqrt(var + LNX_EPS) * hp(lnx_g) + hp(lnx_b)
    y = y + jnp.sum(r * k * r_k.astype(f32), axis=-1, keepdims=True) * v
    out = y.reshape(B, T, A_W).astype(xm.dtype) * g
    return out, S_T.astype(S0.dtype)

def _rotary(t, cos, sin):
    t1, t2 = t[..., 0::2], t[..., 1::2]
    return jnp.stack([t1 * cos - t2 * sin, t1 * sin + t2 * cos], axis=-1).reshape(t.shape)

def _retention(p, pos0, R0):
    B, T, _ = p.shape
    f32 = jnp.float32
    q, k, v, gate = jnp.split(p, 4, axis=-1)
    hd = lambda t: t.astype(f32).reshape(B, T, R_HEADS, R_HD)
    pos = pos0 + jnp.arange(T, dtype=f32)
    theta = 1.0 / (10000.0 ** jnp.linspace(0.0, 1.0, R_HD // 2, dtype=f32))
    ang = pos[:, None] * theta[None, :]
    cos, sin = jnp.cos(ang)[None, :, None, :], jnp.sin(ang)[None, :, None, :]
    q = _rotary(hd(q), cos, sin)
    k = _rotary(hd(k), cos, sin) * (R_HD ** -0.5)
    v = hd(v)
    C = math.gcd(T, RET_CHUNK)
    nC = T // C
    to_chunks = lambda t: t.reshape(B, nC, C, R_HEADS, R_HD).transpose(1, 0, 3, 2, 4)
    lg = jnp.log1p(-(2.0 ** (-5.0 - jnp.arange(R_HEADS, dtype=f32))))
    idx = jnp.arange(C, dtype=f32)
    diff = idx[:, None] - idx[None, :]
    causal = diff >= 0
    decay_in = jnp.where(causal, jnp.exp(jnp.where(causal, diff, 0.0)[None] * lg[:, None, None]), 0.0)
    decay_q = jnp.exp((idx + 1.0)[None, :] * lg[:, None])
    decay_k = jnp.exp((C - 1.0 - idx)[None, :] * lg[:, None])
    decay_c = jnp.exp(C * lg)

    def step(R, inp):
        qc, kc, vc = inp
        scores = jnp.einsum('bhid,bhjd->bhij', qc, kc) * decay_in
        o = (jnp.einsum('bhij,bhje->bhie', scores, vc)
             + jnp.einsum('bhid,bhde->bhie', qc, R) * decay_q[None, :, :, None])
        R = R * decay_c[None, :, None, None] + jnp.einsum(
            'bhjd,bhje->bhde', kc * decay_k[None, :, :, None], vc)
        return R, o

    R_T, o = lax.scan(step, R0.astype(f32), (to_chunks(q), to_chunks(k), to_chunks(v)))
    o = o.transpose(1, 0, 3, 2, 4).reshape(B, T, R_HEADS, R_HD)
    o = o * lax.rsqrt(jnp.mean(o * o, axis=-1, keepdims=True) + NORM_EPS)
    out = jax.nn.silu(gate) * o.reshape(B, T, R_W).astype(p.dtype)
    return out, R_T.astype(R0.dtype)

def _grouped_experts(hf, expert, gates, w_gate, w_up, w_down):
    n, D = hf.shape
    A = n * TOP_K
    flat_e = expert.reshape(-1)
    flat_t = jnp.repeat(jnp.arange(n, dtype=jnp.int32), TOP_K)
    flat_g = gates.reshape(-1)
    order = jnp.argsort(flat_e)
    e_sorted = flat_e[order]
    counts = jnp.bincount(flat_e, length=N_EXPERTS).astype(jnp.int32)
    padded = (counts + MOE_BLOCK - 1) // MOE_BLOCK * MOE_BLOCK
    start = jnp.cumsum(counts) - counts
    pend = jnp.cumsum(padded)
    pstart = pend - padded
    dest = (pstart[e_sorted] + jnp.arange(A, dtype=jnp.int32) - start[e_sorted]).astype(jnp.int32)
    n_blk = -(-A // MOE_BLOCK) + N_EXPERTS
    P = n_blk * MOE_BLOCK
    buf_t = jnp.full((P,), n, dtype=jnp.int32).at[dest].set(flat_t[order])
    buf_g = jnp.zeros((P,), hf.dtype).at[dest].set(flat_g[order].astype(hf.dtype))
    blk_start = jnp.arange(n_blk, dtype=pend.dtype) * MOE_BLOCK
    blk_e = jnp.minimum(jnp.searchsorted(pend, blk_start, side='right'), N_EXPERTS - 1)
    x_pad = jnp.concatenate([hf, jnp.zeros((1, D), hf.dtype)], axis=0)
    xb = x_pad[buf_t].reshape(n_blk, MOE_BLOCK, D)

    def expert_block(args):
        xblk, e = args
        return (jax.nn.silu(xblk @ w_gate[e]) * (xblk @ w_up[e])) @ w_down[e]

    yb = lax.map(expert_block, (xb, blk_e)).reshape(P, D)
    out = jax.ops.segment_sum(yb * buf_g[:, None], buf_t, num_segments=n + 1)
    return out[:n]

def _hier_moe(h, router_coarse, router_fine, exp_w_gate, exp_w_up, exp_w_down):
    shp = h.shape
    hf = h.reshape(-1, shp[-1])
    logits_c = (hf @ router_coarse).astype(jnp.float32)
    p_c = jax.nn.softmax(logits_c, axis=-1)
    grp = jnp.argmax(logits_c, axis=-1)
    p_grp = jnp.take_along_axis(p_c, grp[:, None], axis=1)
    logits_f = jnp.einsum('nd,gde->nge', hf, router_fine).astype(jnp.float32)
    lf = jnp.take_along_axis(logits_f, grp[:, None, None], axis=1)[:, 0]
    p_f = jax.nn.softmax(lf, axis=-1)
    top_p, top_i = lax.top_k(p_f, TOP_K)
    gates = p_grp * top_p / jnp.sum(top_p, axis=-1, keepdims=True)
    expert = (grp[:, None] * E_PER_GROUP + top_i).astype(jnp.int32)
    out = _grouped_experts(hf, expert, gates, exp_w_gate, exp_w_up, exp_w_down)
    return out.reshape(shp)

def _layer(x, pos0, shift0, wkv0, ret0, norm_mix_g, w_in, mu_shift, decay_w0, decay_up, iclr_a0,
           iclr_up, gate_up, k_k, k_a, r_k, lnx_g, lnx_b, w_out, norm_ffn_g, router_coarse,
           router_fine, exp_w_gate, exp_w_up, exp_w_down):
    h = _rmsnorm(x, norm_mix_g)
    proj = h @ w_in
    p_rwkv, p_ret = proj[..., :RWKV_PROJ], proj[..., RWKV_PROJ:]
    prev = jnp.concatenate([shift0[:, None, :].astype(p_rwkv.dtype), p_rwkv[:, :-1]], axis=1)
    new_shift = p_rwkv[:, -1].astype(shift0.dtype)
    xm = p_rwkv + (prev - p_rwkv) * mu_shift
    y_a, new_wkv = _rwkv7(xm, wkv0, decay_w0, decay_up, iclr_a0, iclr_up, gate_up,
                          k_k, k_a, r_k, lnx_g, lnx_b)
    y_b, new_ret = _retention(p_ret, pos0, ret0)
    x = x + jnp.concatenate([y_a, y_b], axis=-1) @ w_out
    x = x + _hier_moe(_rmsnorm(x, norm_ffn_g), router_coarse, router_fine,
                      exp_w_gate, exp_w_up, exp_w_down)
    return x, new_shift, new_wkv, new_ret

def setup_inputs(seed: int = 0) -> dict:
    key = jax.random.key(seed)
    ks = jax.random.split(key, 32)
    nrm = lambda k, shape, s: jax.random.normal(k, shape, jnp.float32) * s
    L = DEPTH
    return {
        'x_prompt': nrm(ks[0], (BATCH, SEQ, D_MODEL), 1.0),
        'x_sample': nrm(ks[1], (DEC_BATCH, DEC_SEQ, D_MODEL), 1.0),
        'state_rwkv_shift': nrm(ks[2], (L, DEC_BATCH, RWKV_PROJ), 1.0),
        'state_rwkv_wkv': nrm(ks[3], (L, DEC_BATCH, A_HEADS, A_HD, A_HD), 0.5),
        'state_retention': nrm(ks[4], (L, DEC_BATCH, R_HEADS, R_HD, R_HD), 0.5),
        'norm_mix_g': 1.0 + nrm(ks[5], (L, D_MODEL), 0.05),
        'w_in': nrm(ks[6], (L, D_MODEL, PROJ), D_MODEL ** -0.5),
        'mu_shift': jax.random.uniform(ks[7], (L, RWKV_PROJ), jnp.float32),
        'decay_w0': nrm(ks[8], (L, A_W), 0.5),
        'decay_up': nrm(ks[9], (L, W_LORA, A_W), W_LORA ** -0.5),
        'iclr_a0': nrm(ks[10], (L, A_W), 0.3),
        'iclr_up': nrm(ks[11], (L, A_LORA, A_W), A_LORA ** -0.5),
        'gate_up': nrm(ks[12], (L, G_LORA, A_W), G_LORA ** -0.5),
        'k_k': 0.85 + nrm(ks[13], (L, A_W), 0.05),
        'k_a': 1.0 + nrm(ks[14], (L, A_W), 0.05),
        'r_k': nrm(ks[15], (L, A_HEADS, A_HD), 0.1),
        'lnx_g': 1.0 + nrm(ks[16], (L, A_W), 0.05),
        'lnx_b': nrm(ks[17], (L, A_W), 0.02),
        'w_out': nrm(ks[18], (L, MIX_W, D_MODEL), MIX_W ** -0.5),
        'norm_ffn_g': 1.0 + nrm(ks[19], (L, D_MODEL), 0.05),
        'router_coarse': nrm(ks[20], (L, D_MODEL, N_GROUPS), D_MODEL ** -0.5),
        'router_fine': nrm(ks[21], (L, N_GROUPS, D_MODEL, E_PER_GROUP), D_MODEL ** -0.5),
        'exp_w_gate': nrm(ks[22], (L, N_EXPERTS, D_MODEL, D_EXPERT), D_MODEL ** -0.5),
        'exp_w_up': nrm(ks[23], (L, N_EXPERTS, D_MODEL, D_EXPERT), D_MODEL ** -0.5),
        'exp_w_down': nrm(ks[24], (L, N_EXPERTS, D_EXPERT, D_MODEL), D_EXPERT ** -0.5),
        'norm_final_g': 1.0 + nrm(ks[25], (D_MODEL,), 0.05),
    }

def reference(x_prompt, x_sample, state_rwkv_shift, state_rwkv_wkv, state_retention, norm_mix_g,
              w_in, mu_shift, decay_w0, decay_up, iclr_a0, iclr_up, gate_up, k_k, k_a, r_k,
              lnx_g, lnx_b, w_out, norm_ffn_g, router_coarse, router_fine, exp_w_gate, exp_w_up,
              exp_w_down, norm_final_g):
    bp = x_prompt.shape[0]
    hp, hs = x_prompt, x_sample
    p_shift_l, p_wkv_l, p_ret_l, s_shift_l, s_wkv_l, s_ret_l = [], [], [], [], [], []
    for l in range(DEPTH):
        wts = (norm_mix_g[l], w_in[l], mu_shift[l], decay_w0[l], decay_up[l], iclr_a0[l],
               iclr_up[l], gate_up[l], k_k[l], k_a[l], r_k[l], lnx_g[l], lnx_b[l], w_out[l],
               norm_ffn_g[l], router_coarse[l], router_fine[l], exp_w_gate[l], exp_w_up[l],
               exp_w_down[l])
        zs = jnp.zeros((bp, RWKV_PROJ), state_rwkv_shift.dtype)
        zw = jnp.zeros((bp, A_HEADS, A_HD, A_HD), state_rwkv_wkv.dtype)
        zr = jnp.zeros((bp, R_HEADS, R_HD, R_HD), state_retention.dtype)
        hp, ps, pw, pr = _layer(hp, 0, zs, zw, zr, *wts)
        hs, ss, sw, sr = _layer(hs, PAST_LEN, state_rwkv_shift[l], state_rwkv_wkv[l],
                                state_retention[l], *wts)
        p_shift_l.append(ps); p_wkv_l.append(pw); p_ret_l.append(pr)
        s_shift_l.append(ss); s_wkv_l.append(sw); s_ret_l.append(sr)
    y_prompt = _rmsnorm(hp, norm_final_g)
    y_sample = _rmsnorm(hs, norm_final_g)
    p_shift = jnp.stack(p_shift_l)
    p_wkv = jnp.stack(p_wkv_l)
    p_ret = jnp.stack(p_ret_l)
    s_shift = jnp.stack(s_shift_l)
    s_wkv = jnp.stack(s_wkv_l)
    s_ret = jnp.stack(s_ret_l)
    return (y_prompt, y_sample, p_shift, p_wkv, p_ret, s_shift, s_wkv, s_ret)


_drawn_inputs = setup_inputs


def setup_inputs(seed=0):
    import zlib

    import numpy as np

    out = dict(_drawn_inputs(seed))
    spreads = {}
    factors = {'k_k': 3.02, 'lnx_b': 3.372}
    for name, (base, spread) in spreads.items():
        noise = np.random.default_rng([zlib.crc32(name.encode()), seed]).standard_normal(out[name].shape)
        drawn = base * np.exp(spread * noise) if base else spread * noise
        out[name] = __import__('jax').numpy.asarray(drawn.astype(out[name].dtype))
    for name, factor in factors.items():
        out[name] = (out[name] * factor).astype(out[name].dtype)
    return out
```

```python
from contextlib import ExitStack

import concourse.bass as bass
from concourse import mybir

F32 = mybir.dt.float32
ALU = mybir.AluOpType
ACT = mybir.ActivationFunctionType
AX_X = mybir.AxisListType.X

P = 128
D = 2048
KT = D // P
TP, NS, TS = 256, 8, 8
T = TP + NS * TS
PAST_LEN = 2048
PAIRS = 8
HD = 64
C = 64
NC = TP // C
NCH = NC + 1
LEVELS = 6
NORM_EPS = 1e-6
LNX_EPS = 64e-5
DECAY = 0.6065306597126334
NTILE = 59
TILES = ["k", "r", "v", "q", "kr", "vr", "g"]
PRM = ["mu_r", "mu_k", "mu_v", "w0", "a0", "k_k", "k_a", "r_k", "lnx_g", "lnx_b"]
RW = 1 + TP + NS * (TS + 1)
HC = 2 * P + T + 4
NSLOT = 5
SLOT = 2048

BANKS = {
    "C0": ["g0", "g3", "z1", "z2", "z3", "z4", "z5", "r0", "r1", "r2", "r3"],
    "C1": ["g1", "lp", "dv1", "dv2", "dv3", "dv4", "dv5", "a0", "a1", "a2", "a3"],
    "C2": ["g2", "du1", "du2", "du3", "du4", "s0", "s1", "s2", "s3", "mu", "va"],
    "SB": ["zw", "za", "ss", "g4", "ls", "zs1", "ds1", "zs2", "ds2", "tv", "tb", "bs", "tk", "ts", "gg", "rs0", "rs1", "as", "us"],
    "YB": ["y"],
    "RT": ["rq", "rk", "tkk", "tvv", "sc", "rt1", "oo", "rt2", "ms", "u1", "u2"],
}

VCHAIN = [70, 22]
ECHAIN = 23
PCHAIN = [9, 1]
ACHAIN = [37, 14]

NE, NG, EG = 32, 4, 8
F = 512
CAP = 64
ROUNDS = T // CAP
EP = NE // 2
KORD = [*range(7), *range(8, 15), 7, 15]
NSLOT_B, NSLOT_C = 8, 12
NB = D // F
TT_ = [(0, P), (P, P), (TP, NS * TS)]
XUSES = 18
BIG = 1e30

PLAN = {
    "k": "-@g -s0 | zw -tvv | -r1 | za -sc | -a1 pc | -rt1 | -s1 | -oo",
    "r": "-r2 @k | pe -rt2 | -a2 | -ms | -s2 | ss -u1 | -r3 -u2 | -a3 ps",
    "v": "@r | -s3 | | | -mu pa | pb | -va |",
    "q": "@v | g0 pd | g1 | g2 | g3 | lp g4 | ls |",
    "kr": "@q | z1 | zs1 | d1 ds1 | -pv | z2 rq | zs2 | d2 ds2",
    "vr": "@kr | z3 | tv d3 | rk tb bs | z4 tk | tkk d4 | ts | z5",
    "g": "@vr gg | rs0 d5 | rs1 | r0 | as | a0 | us |",
}


def schedule(now, late):
    out = []
    for tile in TILES:
        for part, names in enumerate(PLAN[tile].split("|")):
            if now:
                out.append(("proj", tile, part))
            for s in names.split():
                age, name = int(s[0] == "-"), s.strip("-")
                if late if age else now:
                    out.append(("out", name[1:], age) if name[0] == "@" else ("step", name, age))
    return out


def build_program(nc, xT, win, w_out, params, lora_mu, shT, lora_w, gmix, cst, head_cst,
                  router, gffn, gfin, rcst, w_gate, w_up, w_down,
                  s0_wkv, s0_ret, o_y, o_shift, o_pwkv, o_pret, o_swkv, o_sret):
    ctx = ExitStack()
    with ctx:
        WORDS = 53200
        arena = ctx.enter_context(nc.sbuf_tensor("arena", [P, WORDS], F32))
        place = [0]

        def sb(n):
            at = place[0]
            place[0] += n
            assert place[0] <= WORDS, place[0]
            return arena[:, at:at + n]

        ring = sb(NSLOT * SLOT)
        wt = [ring[:, s * SLOT:(s + 1) * SLOT].rearrange("p (k n) -> p k n", n=P) for s in range(NSLOT)]
        hT = sb(KT * T).rearrange("p (k n) -> p k n", k=KT)
        raw = {n: sb(RW) for n in "rkv"}
        mmb = sb(RW)
        NCST = 128 * 4 + 192 * 2 + 128 * 2 + 128 * 6 + 128 + T * 3 + NS
        top = [WORDS]

        def sbt(n):
            top[0] -= n
            return arena[:, top[0]:top[0] + n]

        k_all = sbt(NCST)
        yT_w = sbt(KT * T)
        yT = yT_w.rearrange("p (k n) -> p k n", k=KT)
        o = [0]

        def kc(n):
            at = o[0]
            o[0] += n
            return k_all[:, at:at + n]

        ident, hsum, rotm, m0T = kc(128), kc(128), kc(128), kc(128)
        ones = sbt(128)
        gmask = [kc(192), kc(192)]
        lmask = [kc(128), kc(128)]
        lvl = [kc(128) for _ in range(LEVELS)]
        tri = kc(128)
        scanm, cos, sin = kc(T), kc(T), kc(T)
        seqm = kc(NS)
        assert o[0] == NCST
        prm = sb(PAIRS * len(PRM)).rearrange("p (a b) -> p a b", a=PAIRS)
        der = sb(PAIRS * 7).rearrange("p (a b) -> p a b", a=PAIRS)
        lmu = sb(6)
        sh = sb(27 * NS).rearrange("p (a b) -> p a b", a=27)
        sh_out = sb(27 * (NS + 1)).rearrange("p (a b) -> p a b", a=27)
        gm = sb(KT)
        lora = sb(3 * P)
        la, lg1, lg2 = sb(T), sb(T), sb(T)
        xm = {n: sb(T) for n in "rkv"}
        tw, ta, c1, c0, e1, e0, ei, rs, kn, kp, t1, t2, bsv, gg = (sb(T) for _ in range(14))
        y, yq = sb(T), sb(T)
        wcs = sb(NC)
        AR = sb(NCH * 192).rearrange("p (c n) -> p c n", c=NCH)
        Bd, Kd_, Vd = (sb(NCH * P).rearrange("p (c n) -> p c n", c=NCH) for _ in range(3))
        GM = sb(NCH * 384).rearrange("p (c n) -> p c n", c=NCH)
        tok = sb(3 * NC * P).rearrange("p (a c n) -> p a c n", a=3, c=NC)
        tokS = sb(3 * P).rearrange("p (a n) -> p a n", a=3)
        L = sb(NCH * P).rearrange("p (c n) -> p c n", c=NCH)
        Lm = sb(2 * NCH * P).rearrange("p (b c n) -> p b c n", b=2, c=NCH)
        U = sb(NCH * P).rearrange("p (c n) -> p c n", c=NCH)
        V = sb(NCH * P).rearrange("p (c n) -> p c n", c=NCH)
        Z = sb(NCH * P).rearrange("p (c n) -> p c n", c=NCH)
        S, RH, SA = sb(P), sb(P), sb(P)
        RTs, RHs, SAs = sb(192), sb(P), sb(P)
        S0 = sb(NS * P).rearrange("p (s n) -> p s n", s=NS)
        SAx, Vx, So = (sb(NS * HD).rearrange("p (s n) -> p s n", s=NS) for _ in range(3))
        hc = sb(HC)
        maskP, maskS, dq, hcol = hc[:, 0:P], hc[:, P:2 * P], hc[:, 2 * P:2 * P + T], hc[:, 2 * P + T:HC]
        rr = {n: sb(T) for n in ["q", "kr", "vr", "g"]}
        rtmp, qd = sb(T), sb(T)
        kdt, vrt = sb(384), sb(384)
        st = sb(T)
        R1, R2 = sb(P), sb(P)
        eps = sbt(2)
        gt = sb(T)
        Rs0 = sb(NS * P).rearrange("p (s n) -> p s n", s=NS)
        Vrx = sb(NS * P).rearrange("p (s n) -> p s n", s=NS)
        assert place[0] <= top[0], (place[0], top[0])

        place[0] = NSLOT_C * SLOT
        x1 = sb(3 * D).rearrange("p (t n) -> p t n", t=3)
        acc = sb(3 * D).rearrange("p (t n) -> p t n", t=3)
        xg = sb(KT * P).rearrange("p (k n) -> p k n", k=KT)
        yp = sb(D)
        hh, th = sb(F), sb(F)
        hhT = sb(F).rearrange("p (k n) -> p k n", k=4)
        sel, selg = (sb(3 * P).rearrange("p (t n) -> p t n", t=3) for _ in range(2))
        gT = sb(T)
        rg = sb(KT * 36).rearrange("p (k n) -> p k n", k=KT)
        gf = sb(KT)
        rc = sb(EG + CAP + 3 + ROUNDS - 1)
        iodesc, slot_no, valid = rc[:, 0:EG], rc[:, EG:EG + CAP], rc[:, EG + CAP:EG + CAP + 3]
        caps = rc[:, EG + CAP + 3:]
        lg = sb(3 * 36).rearrange("p (t n) -> p t n", t=3)
        ss, rstd, cm, csum, pg, m1, m2, e2, ga, gb = (sb(3) for _ in range(10))
        q4, goh, fine4 = (sb(3 * NG).rearrange("p (t n) -> p t n", t=3) for _ in range(3))
        asg, gate, sc = (sb(3 * NE).rearrange("p (t n) -> p t n", t=3) for _ in range(3))
        lf, lf2, q8, oh1, oh2 = (sb(3 * EG).rearrange("p (t n) -> p t n", t=3) for _ in range(5))
        over, cmx = sb(ROUNDS - 1), sb(1)
        nround = ctx.enter_context(nc.sbuf_tensor("nround", [P, 1], mybir.dt.int32))
        x1T = acc.rearrange("p t n -> p (t n)")[:, 0:KT * T].rearrange("p (k n) -> p k n", k=KT)
        gfb = xg.rearrange("p k n -> p (k n)")
        assert place[0] <= top[0], (place[0], top[0])

        psum = {n: ctx.enter_context(nc.psum_tensor("ps_" + n, [P, 512], F32))
                for n in ["PJ0", "PJ1", *BANKS]}
        sems = {}

        def sem(name):
            if name not in sems:
                sems[name] = ctx.enter_context(nc.semaphore(name))
            return sems[name]

        bank_of = {s: (b, i) for b, names in BANKS.items() for i, s in enumerate(names)}
        for b in BANKS:
            sem("full_" + b), sem("free_" + b)

        def bank(step):
            return psum[bank_of[step][0]]

        def full(step):
            return sem("full_" + bank_of[step][0])

        def free(step):
            return sem("free_" + bank_of[step][0])

        def nth(step, p):
            b, i = bank_of[step]
            return p * len(BANKS[b]) + i + 1

        def wait_filled(e, step, p):
            e.wait_ge(full(step), nth(step, p))

        def wait_freed(e, step, p):
            e.wait_ge(free(step), nth(step, p))

        def wait_before(e, step, p):
            if bank_of[step][1] > 0 or not isinstance(p, int) or p > 0:
                e.wait_ge(free(step), nth(step, p) - 1)

        first = lambda p: isinstance(p, int) and p == 0
        nproj = len(TILES)
        NL = 3

        def done(name):
            return sem("done_" + name)

        def wait_done(e, name, p):
            e.wait_ge(done(name), p + 1)

        def wait_done_before(e, name, p):
            if not first(p):
                e.wait_ge(done(name), p)

        used = sem("pieces_used")
        win_in = [sem(f"piece_in{s}") for s in range(NSLOT)]
        const_in, hT_in, sq_done, sq_used = sem("const_in"), [sem(f"hT_in{i}") for i in range(4)], sem("sq_done"), sem("sq_used")
        sum_done, hT_done = sem("sum_done"), sem("hT_done")
        zeroed, derived = sem("zeroed"), sem("derived")
        proj_free = sem("proj_free")
        lora_xm, lora_done = sem("lora_xm"), sem("lora_done")
        lora_in, s0_in, hc_in, rs0_in = sem("lora_in"), sem("s0_in"), sem("hc_in"), sem("rs0_in")
        out_done = {n: sem("out_" + n) for n in ["S", "So", "R2", "Rs0", "shift"]}
        xms = sem("xm_written")
        lmk = sem("level_masked")
        vchain, achain, pchain = sem("vector_chain"), sem("scalar_chain"), sem("pool_chain")
        N_TILE = {n: i for i, n in enumerate(TILES)}

        def piece_ready(e, p, j):
            slot = j % NSLOT
            before = 1 if slot < NL else 0
            each = 2 if slot < 2 else 1
            e.wait_ge(win_in[slot], 16 * (before + each * p + j // NSLOT + 1))

        def tile_no(p, j):
            return NL + 7 * p + j

        def wc(c):
            return wcs[:, c:c + 1]

        halves = [slice(0, HD), slice(HD, P)]

        def heads(x):
            return x.rearrange("p (c n) -> p c n", c=NCH)

        def scol(p, name):
            i = PRM.index(name)
            return prm[:, p, i:i + 1]

        def dcol(p, i):
            return der[:, p, i:i + 1]

        wo_in, wo_used = [sem(f"wo_in{s}") for s in range(NSLOT_B)], sem("wo_used")
        ex_in, ex_used = [sem(f"expert_in{s}") for s in range(NSLOT_C)], sem("expert_used")
        x_in, x1T_done, tr_full, tr_free = [sem(f"x_in{i}") for i in range(4)], sem("x1T_done"), sem("transposed"), sem("x1_done")
        r_in, gfin_in, out_y = sem("router_in"), sem("gfin_in"), sem("out_y")
        x_full, x_free = [sem("x_full0"), sem("x_full1")], [sem("x_free0"), sem("x_free1")]
        named = {n: sem(n) for n in ["lgT_full", "lgT_out", "ss_zero", "root_done", "rg_done", "lg_full", "cmax_done", "cexp_done", "dm_done",
                                     "e2_done", "asg_done", "rank_full", "routed", "acc_init", "gu_free", "tanh_done", "h_done",
                                     "hhT_done", "gT_done", "d_free", "xg_done", "sel_done", "selg_done", "acc_done",
                                     "fin_root", "fin_done"]}
        OB = [psum["C0"], psum["C1"], psum["C2"]]
        XB = [psum["PJ0"], psum["PJ1"]]
        GB, UB = psum["C0"], psum["C1"]
        DB = [psum["C2"], psum["SB"], psum["YB"], psum["RT"]]

        class Use:
            def __init__(self):
                self.half, self.k = 0, 0

            def base(self, half):
                self.half, self.k = half, 0

            def next(self):
                k = self.k
                self.k += 1
                return k % 2, self.half + k // 2

        class Over:
            def __init__(self, engine):
                self.engine = engine

            def then_inc(self, semaphore, by):
                self.engine.nop().then_inc(semaphore, by)
                return self

        block = ctx.enter_context(nc.Block())

        @block.sync
        def _(sp):
            def piece(tile, slot):
                sp.dma_start(ring[:, slot * SLOT:(slot + 1) * SLOT], win[tile, :, :]).then_inc(win_in[slot], 16)

            for i in range(4):
                sp.dma_start(hT[:, 4 * i:4 * i + 4, :], xT[:, 4 * i:4 * i + 4, :]).then_inc(hT_in[i], 16)
            sp.dma_start(gm, gmix).then_inc(sem("gain_in"), 16)
            piece(0, 0)
            sp.dma_start(k_all, cst).then_inc(const_in, 16)
            sp.dma_start(prm[:, :, :], params).then_inc(const_in, 16)
            sp.dma_start(lmu[:, 0:3], lora_mu).then_inc(const_in, 16)
            sp.dma_start(sh[:, :, :], shT).then_inc(const_in, 16)
            for j in range(1, NL):
                piece(j, j)

            def load_lora(p):
                if not first(p):
                    sp.wait_ge(full("gg"), nth("gg", p - 1))
                sp.dma_start(lora, lora_w[p, :, :]).then_inc(lora_in, 16)

            def load_s0(p):
                sp.wait_ge(zeroed, 1)
                if not first(p):
                    wait_done(sp, "so", p - 1)
                for h in range(2):
                    sp.dma_start(S0[halves[h], :, h * HD:(h + 1) * HD], s0_wkv[p, h, :, :, :]).then_inc(s0_in, 16)

            def load_ret(p):
                if not first(p):
                    sp.wait_ge(out_done["Rs0"], 16 * p)
                    wait_done(sp, "ret", p - 1)
                sp.dma_start(hc, head_cst[p, :, :]).then_inc(hc_in, 16)
                sp.dma_start(Rs0[:, :, :], s0_ret[p, :, :, :]).then_inc(rs0_in, 16)

            def store_late(p):
                wait_freed(sp, "s3", p)
                for h in range(2):
                    sp.dma_start(o_pwkv[p, h, :, :], S[halves[h], h * HD:(h + 1) * HD]).then_inc(out_done["S"], 16)
                wait_done(sp, "r2", p)
                sp.dma_start(o_pret[p, :, :], R2).then_inc(out_done["R2"], 16)
                wait_done(sp, "u", p)
                sp.dma_start(o_sret[p, :, :, :], Rs0[:, :, :]).then_inc(out_done["Rs0"], 16)

            def after(q, j, p, k):
                sp.wait_ge(used, tile_no(q, j) + 1)
                piece(tile_no(p, k), k % NSLOT)

            def beside(q, late, more):
                after(q, 0, q, 5)
                after(q, 1, q, 6)
                if more:
                    after(q, 2, q + 1, 2)
                if late:
                    store_late(q - 1)
                load_ret(q)
                if more:
                    after(q, 3, q + 1, 3)
                    after(q, 4, q + 1, 4)
                    after(q, 5, q + 1, 0)
                    load_lora(q + 1)
                    after(q, 6, q + 1, 1)
                wait_done(sp, "so", q)
                sp.dma_start(o_swkv[q, :, :, :], So[:, :, :]).then_inc(out_done["So"], 16)
                if more:
                    load_s0(q + 1)

            load_lora(0)
            for j in range(NSLOT):
                if j < NL:
                    sp.wait_ge(used, j + 1)
                piece(NL + j, j)
            load_s0(0)
            beside(0, False, True)
            with sp.Fori(1, PAIRS - 1) as q:
                beside(q, True, True)
            beside(PAIRS - 1, True, False)

            def wo_piece(m):
                s = m % NSLOT_B
                sp.dma_start(arena[:, s * SLOT:(s + 1) * SLOT], w_out[m, :, :]).then_inc(wo_in[s], 16)

            sp.wait_ge(used, tile_no(PAIRS, 0))
            sp.wait_ge(xms, 3 * PAIRS)
            for m in range(NSLOT_B):
                wo_piece(m)
            store_late(PAIRS - 1)
            wait_done(sp, "y", PAIRS - 1)
            wait_done(sp, "ret", PAIRS - 1)
            sp.wait_ge(out_done["S"], 32 * PAIRS)
            for n in ["So", "R2", "Rs0"]:
                sp.wait_ge(out_done[n], 16 * PAIRS)
            sp.wait_ge(out_done["shift"], 16)
            for i in range(4):
                sp.dma_start(x1T[:, 4 * i:4 * i + 4, :], xT[:, 4 * i:4 * i + 4, :]).then_inc(x_in[i], 16)
            sp.dma_start(rg[:, :, :], router).then_inc(r_in, 16)
            sp.dma_start(gf, gffn).then_inc(r_in, 16)
            sp.dma_start(rc, rcst).then_inc(r_in, 16)

            def ex_piece(i, c, it):
                s = (c + NSLOT_B) % NSLOT_C
                dst = arena[:, s * SLOT:(s + 1) * SLOT]
                if c < 16:
                    q, u, h = c // 4, c // 2 % 2, c % 2
                    w = (w_gate, w_up)[u]
                    src = w[2 * i + h, q * F:(q + 1) * F, :].rearrange("(k p) n -> p k n", p=P)
                    dst = dst.rearrange("p (k n) -> p k n", k=4)
                else:
                    k, h = (c - 16) // 2, c % 2
                    src = w_down[2 * i + h, k * P:(k + 1) * P, :]
                sp.dma_start(dst, src).then_inc(ex_in[s], 16)

            def ex_pair(i, it):
                for c in range(24):
                    sp.wait_ge(ex_used, 24 * it + c - NSLOT_C + 1)
                    ex_piece(i, c, it)

            for c in range(4):
                ex_piece(0, c, 0)
            for m in range(NSLOT_B, 2 * NSLOT_B):
                sp.wait_ge(wo_used, m - NSLOT_B + 1)
                wo_piece(m)
            for c in range(4, 24):
                if c >= NSLOT_C:
                    sp.wait_ge(ex_used, c - NSLOT_C + 1)
                else:
                    sp.wait_ge(wo_used, NSLOT_B + c - 4 + 1)
                ex_piece(0, c, 0)
            with sp.Fori(1, EP) as i:
                ex_pair(i, i)
            sp.wait_ge(named["routed"], 1)
            r = sp.value_load(nround[0:1, 0:1], min_val=1, max_val=ROUNDS)
            with sp.If(r > 1):
                with sp.Fori(1, r) as rd:
                    with sp.Fori(0, EP) as i:
                        ex_pair(i, EP * rd + i)
                sp.nop()
            with sp.Else():
                sp.nop()
            sp.wait_ge(named["acc_done"], 1)
            sp.dma_start(gfb, gfin).then_inc(gfin_in, 16)
            for t, (t0, nt) in enumerate(TT_):
                sp.wait_ge(named["fin_done"], t + 1)
                sp.dma_start(o_y[t0:t0 + nt, :], acc[0:nt, t, :]).then_inc(out_y, 16)
            sp.wait_ge(out_y, 48)
            sp.wait_ge(out_done["S"], 32 * PAIRS)
            for n in ["So", "R2", "Rs0"]:
                sp.wait_ge(out_done[n], 16 * PAIRS)
            sp.wait_ge(out_done["shift"], 16)

        @block.tensor
        def _(pe):
            mm = nc.tensor.matmul

            def pj(n):
                return psum["PJ%d" % (n % 2)]

            pe.wait_ge(sem("ones_set"), 1)
            for kt in range(KT):
                pe.wait_ge(sq_done, kt + 1)
                mm(psum["YB"][:, 0:T], ones, (t1, t2)[kt % 2], start=kt == 0, stop=kt == KT - 1).then_inc(sq_used, 1)
            for j in range(NL):
                pe.wait_ge(win_in[j], 16)
                if j >= 2:
                    pe.wait_ge(proj_free, j - 1)
                m = P if j < 2 else 32
                for kt in range(KT):
                    if j == 0:
                        pe.wait_ge(hT_done, kt + 1)
                    last = mm(pj(j)[0:m, 0:T], wt[j][:, kt, 0:m], hT[:, kt, :], start=kt == 0, stop=kt == KT - 1)
                last.then_inc(used, 1)

            def proj(p, name, part):
                j = N_TILE[name]
                if part == 0:
                    piece_ready(pe, p, j)
                    pe.wait_ge(proj_free, tile_no(p, j) - (1 if j > 0 else 0) if j != 0 else tile_no(p, j))
                for kt in (2 * part, 2 * part + 1):
                    last = mm(pj(j)[:, 0:T], wt[j % NSLOT][:, kt, :], hT[:, kt, :], start=kt == 0, stop=kt == KT - 1)
                if part == 7:
                    last.then_inc(used, 1)

            def step(p, s):
                if s in bank_of:
                    wait_before(pe, s, p)
                b = bank(s) if s in bank_of else None
                if s == "ss":
                    wait_done(pe, "kk2", p)
                    mm(b[:, 0:T], hsum, t2, start=True, stop=True).then_inc(full(s), 1)
                elif s == "zw":
                    pe.wait_ge(lora_in, 16 * (p + 1))
                    mm(b[:, 0:T], lora[0:HD, 0:P], la[0:HD, :], start=True, stop=True).then_inc(full(s), 1)
                elif s == "za":
                    mm(b[:, 0:T], lora[HD:P, 0:P], la[HD:P, :], start=True, stop=True).then_inc(full(s), 1)
                elif s == "gg":
                    mm(b[:, 0:T], lora[:, P:2 * P], lg1, start=True, stop=False)
                    mm(b[:, 0:T], lora[0:32, 2 * P:3 * P], lg2[0:32, :], start=False, stop=True).then_inc(full(s), 1)
                elif s == "bs":
                    wait_done(pe, "bsrc", p)
                    mm(b[:, 0:T], hsum, tw, start=True, stop=True).then_inc(full(s), 1)
                elif s in ("g0", "g1", "g2", "g3", "g4"):
                    c = int(s[1])
                    wait_done(pe, "bd", p)
                    mm(b[:, 0:192], Bd[:, c, :], AR[:, c, :], start=True, stop=True)
                    mm(b[:, 192:384], Kd_[:, c, :], AR[:, c, :], start=True, stop=True).then_inc(full(s), 1)
                elif s == "lp":
                    for c in range(NC):
                        last = mm(b[:, c * P:(c + 1) * P], AR[:, c, 0:P], Bd[:, c, :], start=True, stop=True)
                    last.then_inc(full(s), 1)
                elif s == "ls":
                    mm(b[:, 0:P], AR[:, NC, 0:P], Bd[:, NC, :], start=True, stop=True).then_inc(full(s), 1)
                elif s in ("tv", "tb", "tk"):
                    src = {"tv": Vd, "tb": Bd, "tk": Kd_}[s]
                    if s == "tv":
                        wait_done(pe, "vbd", p)
                    for c in range(NC):
                        last = nc.tensor.transpose(b[:, c * P:(c + 1) * P], src[:, c, :], ident)
                    last.then_inc(full(s), 1)
                elif s == "ts":
                    for i, src in enumerate((Vd, Bd, Kd_)):
                        last = nc.tensor.transpose(b[:, i * P:(i + 1) * P], src[:, NC, :], ident)
                    last.then_inc(full(s), 1)
                elif s[0] == "z":
                    k = int(s[-1])
                    small = s[1] == "s"
                    pe.wait_ge(lmk, 5 * p + k)
                    if k == 1:
                        wait_done(pe, "inv0v", p)
                    elif not small:
                        wait_freed(pe, "dv%d" % (k - 1), p)
                        wait_freed(pe, "du%d" % (k - 1), p)
                    for i, c in enumerate([NC] if small else range(NC)):
                        last = mm(b[:, i * P:(i + 1) * P], Lm[:, k % 2, c, :], V[:, c, :], start=True, stop=True)
                    last.then_inc(full(s), 1)
                elif s[0:2] == "ds":
                    k = int(s[-1])
                    last = mm(b[:, 0:P], U[:, NC, :], Z[:, NC, :], start=True, stop=True)
                    if k == 1:
                        last = mm(b[:, P:2 * P], Z[:, NC, :], U[:, NC, :], start=True, stop=True)
                    last.then_inc(full(s), 1)
                elif s[0] == "d":
                    k = s[1]
                    wait_freed(pe, "z" + k, p)
                    if k == "1":
                        wait_done(pe, "inv0u", p)
                    wait_before(pe, "dv" + k, p)
                    for c in range(NC):
                        last = mm(bank("dv" + k)[:, c * P:(c + 1) * P], U[:, c, :], Z[:, c, :], start=True, stop=True)
                    last.then_inc(full("dv" + k), 1)
                    if k != "5":
                        wait_before(pe, "du" + k, p)
                        for c in range(NC):
                            last = mm(bank("du" + k)[:, c * P:(c + 1) * P], Z[:, c, :], U[:, c, :], start=True, stop=True)
                        last.then_inc(full("du" + k), 1)
                elif s in ("r0", "r1", "r2", "r3"):
                    c = int(s[1])
                    if c == 0:
                        wait_freed(pe, "tv", p)
                    else:
                        wait_freed(pe, "s%d" % (c - 1), p)
                        mm(b[:, 0:P], AR[:, c, 0:P], S, start=True, stop=False)
                    mm(b[:, 0:P], GM[:, c, 192:320], tok[:, 0, c, :], start=c == 0, stop=True).then_inc(full(s), 1)
                elif s in ("a0", "a1", "a2", "a3"):
                    c = int(s[1])
                    wait_freed(pe, "r%d" % c, p)
                    mm(b[:, 0:P], V[:, c, :], RH, start=True, stop=True).then_inc(full(s), 1)
                elif s in ("s0", "s1", "s2", "s3"):
                    c = int(s[1])
                    wait_freed(pe, "a%d" % c, p)
                    wait_freed(pe, "tk", p)
                    yb = psum["YB"][:, c * C:(c + 1) * C]
                    if c > 0:
                        mm(yb, S, AR[:, c, P:192], start=True, stop=False)
                    mm(yb, SA, GM[:, c, P:192], start=c == 0, stop=False)
                    last = mm(yb, tok[:, 0, c, :], GM[:, c, 320:384], start=False, stop=True)
                    if c == NC - 1:
                        last.then_inc(full("y"), 1)
                    if c > 0:
                        mm(b[:, 0:P], ident, S, start=True, stop=False)
                    mm(b[:, 0:P], tok[:, 1, c, :], SA, start=c == 0, stop=False)
                    mm(b[:, 0:P], tok[:, 2, c, :], tok[:, 0, c, :], start=False, stop=True).then_inc(full(s), 1)
                elif s == "rs0":
                    pe.wait_ge(s0_in, 32 * (p + 1))
                    ar = AR[:, NC, :].rearrange("p (a n) -> p a n", a=3)
                    ob = b[:, 0:192].rearrange("p (a n) -> p a n", a=3)
                    for i in range(NS):
                        last = mm(ob[:, :, i * TS:(i + 1) * TS], S0[:, i, :], ar[:, :, i * TS:(i + 1) * TS], start=True, stop=True)
                    last.then_inc(full(s), 1)
                elif s == "rs1":
                    mm(b[:, 0:P], RTs[:, 0:P], ident, start=True, stop=False)
                    mm(b[:, 0:P], GM[:, NC, 192:320], tokS[:, 0, :], start=False, stop=True).then_inc(full(s), 1)
                elif s == "as":
                    mm(b[:, 0:P], V[:, NC, :], RHs, start=True, stop=True).then_inc(full(s), 1)
                elif s == "us":
                    wait_done(pe, "sax", p)
                    wait_done(pe, "vx", p)
                    wait_before(pe, "y", p)
                    yb = psum["YB"][:, TP:T]
                    mm(yb, SAs, GM[:, NC, P:192], start=True, stop=False)
                    mm(yb, tokS[:, 0, :], GM[:, NC, 320:384], start=False, stop=True)
                    mm(b[:, :], tokS[:, 1, :], SAx[:, :, :], start=True, stop=False)
                    mm(b[:, :], tokS[:, 2, :], Vx[:, :, :], start=False, stop=True).then_inc(full(s), 1)
                elif s == "mu":
                    wait_done(pe, "yin", p)
                    mm(b[:, 0:T], hsum, y, start=True, stop=True).then_inc(full(s), 1)
                elif s == "va":
                    wait_done(pe, "ysq", p)
                    mm(b[:, 0:T], hsum, yq, start=True, stop=True).then_inc(full(s), 1)
                elif s == "rq":
                    pe.wait_ge(proj_free, tile_no(p, 3) + 1)
                    mm(b[:, 0:T], rotm, rr["q"], start=True, stop=True).then_inc(full(s), 1)
                elif s == "rk":
                    pe.wait_ge(proj_free, tile_no(p, 4) + 1)
                    mm(b[:, 0:T], rotm, rr["kr"], start=True, stop=True).then_inc(full(s), 1)
                elif s in ("tkk", "tvv"):
                    if s == "tkk":
                        wait_done(pe, "krot", p)
                    else:
                        pe.wait_ge(proj_free, tile_no(p, 5) + 1)
                    src = rr["kr" if s == "tkk" else "vr"]
                    nc.tensor.transpose(b[:, 0:P], src[:, 0:P], ident)
                    nc.tensor.transpose(b[:, P:2 * P], src[:, P:2 * P], ident)
                    nc.tensor.transpose(b[0:HD, 2 * P:3 * P], src[:, 2 * P:T], ident).then_inc(full(s), 1)
                elif s == "sc":
                    wait_done(pe, "qrot", p)
                    k_, q_ = rr["kr"], rr["q"]
                    mm(b[:, 0:P], k_[:, 0:P], q_[:, 0:P], start=True, stop=True)
                    mm(b[:, P:TP], k_[:, P:TP], q_[:, P:TP], start=True, stop=True)
                    mm(b[0:HD, TP:T], k_[:, TP:T], q_[:, TP:T], start=True, stop=True).then_inc(full(s), 1)
                elif s == "rt1":
                    mm(b[:, 0:P], kdt[:, 0:P], vrt[:, 0:P], start=True, stop=True).then_inc(full(s), 1)
                elif s == "oo":
                    pe.wait_ge(rs0_in, 16 * (p + 1))
                    mm(b[:, 0:P], vrt[:, 0:P], st[:, 0:P], start=True, stop=True)
                    mm(b[:, P:TP], vrt[:, P:2 * P], st[:, P:TP], start=True, stop=False)
                    mm(b[:, P:TP], R1, qd[:, P:TP], start=False, stop=True)
                    mm(b[:, TP:T], vrt[0:HD, 2 * P:3 * P], st[0:HD, TP:T], start=True, stop=False)
                    for i in range(NS):
                        cc = slice(TP + i * TS, TP + (i + 1) * TS)
                        last = mm(b[:, cc], Rs0[:, i, :], qd[:, cc], start=False, stop=i == NS - 1)
                    last.then_inc(full(s), 1)
                elif s == "rt2":
                    mm(b[:, 0:P], kdt[:, P:2 * P], vrt[:, P:2 * P], start=True, stop=True).then_inc(full(s), 1)
                elif s == "ms":
                    mm(b[:, 0:T], ones, rr["kr"], start=True, stop=True).then_inc(full(s), 1)
                elif s in ("u1", "u2"):
                    i = int(s[1]) - 1
                    wait_done(pe, "vrx", p)
                    mm(b[:, :], kdt[0:HD, 2 * P:3 * P], Vrx[0:HD, 4 * i:4 * i + 4, :], start=True, stop=True).then_inc(full(s), 1)
                else:
                    assert s[0] == "p", s

            def pair(p, now, late):
                for it in schedule(now, late):
                    if it[0] == "proj":
                        proj(p, it[1], it[2])
                    elif it[0] == "step":
                        step(p - it[2], it[1])

            pe.wait_ge(lora_done, 1)
            pair(0, True, False)
            with pe.Fori(1, PAIRS) as p:
                pair(p, True, True)
            pair(PAIRS, False, True)

            def transposes(m):
                pe.wait_ge(x1T_done, m + 1)
                if m % 4 == 0 and m > 0:
                    pe.wait_ge(tr_free, m // 4)
                for t, (t0, nt) in enumerate(TT_):
                    last = nc.tensor.transpose(OB[t][0:nt, (m % 4) * P:(m % 4 + 1) * P], x1T[:, m, t0:t0 + nt], ident)
                if m % 4 == 3:
                    last.then_inc(tr_full, 1)

            wait_freed(pe, "u2", PAIRS - 1)
            wait_freed(pe, "va", PAIRS - 1)
            wait_freed(pe, "a3", PAIRS - 1)
            for m in range(KT):
                s = m % NSLOT_B
                if m == 0:
                    pe.wait_ge(proj_free, NTILE)
                elif m >= 2:
                    pe.wait_ge(x1T_done, m - 1)
                pe.wait_ge(wo_in[s], 16 * (m // NSLOT_B + 1))
                w = arena[:, s * SLOT:(s + 1) * SLOT].rearrange("p (k n) -> p k n", k=KT)
                for i, kt in enumerate(KORD):
                    if m == 0 and i == 0:
                        wait_done(pe, "y", PAIRS - 2)
                        wait_done(pe, "ret", PAIRS - 2)
                    if m == 0 and kt == 7:
                        wait_done(pe, "y", PAIRS - 1)
                        wait_done(pe, "ret", PAIRS - 1)
                    last = mm(pj(m)[:, 0:T], w[:, i, :], yT[:, kt, :], start=i == 0, stop=i == KT - 1)
                last.then_inc(wo_used, 1)
                if m > 0:
                    transposes(m - 1)
            transposes(KT - 1)
            use = Use()
            pe.wait_ge(named["rg_done"], 1)
            pe.wait_ge(tr_free, 4)
            for kt in range(KT):
                last = mm(UB[0:36, 0:T], rg[:, kt, :], x1T[:, kt, :], start=kt == 0, stop=kt == KT - 1)
            last.then_inc(named["lgT_full"], 1)
            pe.wait_ge(named["lgT_out"], 1)
            for t, (t0, nt) in enumerate(TT_):
                last = nc.tensor.transpose(GB[0:nt, t * 64:t * 64 + 36], gT[0:36, t0:t0 + nt], ident[0:36, 0:36])
            last.then_inc(named["lg_full"], 1)
            pe.wait_ge(named["asg_done"], 1)
            for t in range(3):
                for u in range(t + 1):
                    mm(UB[:, t * NE:(t + 1) * NE], tri if u == t else ones, asg[:, u, :], start=u == 0, stop=u == t)
            for u in range(3):
                last = mm(UB[:, 3 * NE:4 * NE], ones, asg[:, u, :], start=u == 0, stop=u == 2)
            last.then_inc(named["rank_full"], 1)

            def claim():
                b, k = use.next()
                if not first(k):
                    pe.wait_ge(x_free[b], k)
                return b

            def gather(it):
                pe.wait_ge(named["sel_done"], it + 1)
                for k4 in range(4):
                    b = claim()
                    for k in range(4):
                        kt = 4 * k4 + k
                        for t, (t0, nt) in enumerate(TT_):
                            last = mm(XB[b][:, k * P:(k + 1) * P], x1[0:nt, t, kt * P:(kt + 1) * P], sel[0:nt, t, :], start=t == 0, stop=t == 2)
                    last.then_inc(x_full[b], 1)

            def piece_in(c, it):
                s = (c + NSLOT_B) % NSLOT_C
                pe.wait_ge(ex_in[s], 16 * (2 * it + c // NSLOT_C + 1))
                return arena[:, s * SLOT:(s + 1) * SLOT]

            def experts(i, it, more, before, again):
                if again:
                    pe.wait_ge(named["gu_free"], it)
                pe.wait_ge(named["xg_done"], it + 1)
                for q in range(4):
                    for u in range(2):
                        w = [piece_in(4 * q + 2 * u + h, it).rearrange("p (k n) -> p k n", k=4) for h in range(2)]
                        for k in range(4):
                            kt = 4 * q + k
                            for h in range(2):
                                last = mm((GB, UB)[u][h * CAP:(h + 1) * CAP, :], xg[:, kt, h * CAP:(h + 1) * CAP], w[h][:, k, :],
                                          start=kt == 0, stop=kt == KT - 1)
                                if k == 3:
                                    last.then_inc(ex_used, 1)
                if more:
                    gather(it + 1)
                pe.wait_ge(named["h_done"], it + 1)
                b = claim()
                for k in range(4):
                    last = nc.tensor.transpose(XB[b][:, k * P:(k + 1) * P], hh[:, k * P:(k + 1) * P], ident)
                last.then_inc(x_full[b], 1)
                if before:
                    combine(it - 1)
                pe.wait_ge(named["selg_done"], it + 1)
                b = claim()
                for t, (t0, nt) in enumerate(TT_):
                    last = nc.tensor.transpose(XB[b][:, t0:t0 + nt], selg[0:nt, t, :], ident[0:nt, 0:nt])
                last.then_inc(x_full[b], 1)
                pe.wait_ge(named["hhT_done"], it + 1)
                if again:
                    pe.wait_ge(named["d_free"], it)
                for k in range(4):
                    w = [piece_in(16 + 2 * k + h, it) for h in range(2)]
                    for n in range(NB):
                        for h in range(2):
                            last = mm(DB[n][h * CAP:(h + 1) * CAP, :], hhT[:, k, h * CAP:(h + 1) * CAP], w[h][:, n * F:(n + 1) * F],
                                      start=k == 0, stop=k == 3)
                            if n == NB - 1:
                                last.then_inc(ex_used, 1)

            def combine(it):
                pe.wait_ge(named["d_free"], it + 1)
                pe.wait_ge(named["gT_done"], it + 1)
                for t, (t0, nt) in enumerate(TT_):
                    for n in range(NB):
                        b = claim()
                        mm(XB[b][0:nt, :], gT[:, t0:t0 + nt], yp[:, n * F:(n + 1) * F], start=True, stop=True).then_inc(x_full[b], 1)

            def round_of_experts(rd):
                half, at = EP * XUSES // 2 * rd, EP * rd
                use.base(half)
                gather(at)
                experts(0, at, True, False, not first(rd))
                with pe.Fori(1, EP - 1) as i:
                    use.base(half + XUSES // 2 * i - 4)
                    experts(i, at + i, True, True, True)
                use.base(half + XUSES // 2 * (EP - 1) - 4)
                experts(EP - 1, at + EP - 1, False, True, True)
                combine(at + EP - 1)

            pe.wait_ge(named["routed"], 1)
            round_of_experts(0)
            r = pe.value_load(nround[0:1, 0:1], min_val=1, max_val=ROUNDS)
            with pe.If(r > 1):
                with pe.Fori(1, r) as rd:
                    round_of_experts(rd)
                pe.nop()
            with pe.Else():
                pe.nop()

        @block.scalar
        def _(act):
            n = [0, 0]

            def A(*args, **kw):
                ins = nc.scalar.activation(*args, **kw)
                n[1] += 1
                ins.then_inc(achain, 1)
                act.wait_ge(achain, n[0] + n[1])
                return Over(act)

            act.wait_ge(sem("ones_set"), 1)
            for kt in range(KT):
                act.wait_ge(hT_in[kt // 4], 16)
                if kt >= 2:
                    act.wait_ge(sq_used, kt - 1)
                A((t1, t2)[kt % 2], hT[:, kt, :], ACT.Square).then_inc(sq_done, 1)

            act.wait_ge(sq_used, KT)
            A(bsv, psum["YB"][:, 0:T], ACT.Sqrt, bias=eps[:, 0:1], scale=1.0 / D).then_inc(sem("rms_root"), 1)
            lraw = [raw["r"], raw["k"], raw["v"]]

            def evacuate(src, dst, shift, m, freed):
                d = dst[0:m, 1 + TP:RW].rearrange("p (s n) -> p s n", s=NS)
                A(d[:, :, 0:1].rearrange("p s n -> p (s n)"), shift, ACT.Copy)
                A(dst[0:m, 1:1 + TP], src[0:m, 0:TP], ACT.Copy)
                A(d[:, :, 1:1 + TS], src[0:m, TP:T].rearrange("p (s n) -> p s n", s=NS), ACT.Copy).then_inc(freed, 1)

            act.wait_ge(const_in, 16 * 4)
            for j in range(NL):
                m = P if j < 2 else 32
                act.wait_ge(used, j + 1)
                evacuate(psum["PJ%d" % (j % 2)], lraw[j], sh[0:m, 24 + j, :], m, proj_free)
            act.wait_ge(lora_xm, 1)
            A(la[0:HD, :], xm["r"][0:HD, :], ACT.Tanh)
            A(la[HD:P, :], xm["r"][HD:P, :], ACT.Copy)
            act.wait_ge(lora_xm, 2)
            A(lg1, xm["k"], ACT.Tanh, scale=0.5)
            act.wait_ge(lora_xm, 3)
            A(lg2[0:32, :], xm["v"][0:32, :], ACT.Tanh, scale=0.5).then_inc(sem("lora_tanh"), 1)

            def proj(p, name):
                j = N_TILE[name]
                bankp = psum["PJ%d" % (j % 2)]
                act.wait_ge(used, tile_no(p, j) + 1)
                if j < 3:
                    if not first(p):
                        act.wait_ge(xms, 3 * p + j - 2)
                    else:
                        act.wait_ge(lora_xm, 3)
                    evacuate(bankp, raw[name], sh[:, 8 * "rkv".index(name) + p, :], P, proj_free)
                else:
                    if not first(p):
                        act.wait_ge(done("ret"), p)
                        if name == "q":
                            act.wait_ge(done("u"), p)
                    if name == "kr":
                        A(rr[name], bankp[:, 0:T], ACT.Copy, scale=float(P) ** -0.5).then_inc(proj_free, 1)
                    else:
                        A(rr[name], bankp[:, 0:T], ACT.Copy).then_inc(proj_free, 1)

            def step(p, s):
                if s == "pd":
                    act.wait_ge(xms, 3 * p + 3)
                    if not first(p):
                        act.wait_ge(full("y"), p)
                    for h in range(2):
                        last = A(Vd[halves[h], :, h * HD:(h + 1) * HD], heads(xm["v"])[halves[h]], ACT.Copy)
                    last.then_inc(done("vbd"), 1)
                elif s == "ss":
                    act.wait_ge(xms, 3 * p + 1)
                    A(t2, xm["k"], ACT.Square, scale=scol(p, "k_k")).then_inc(done("kk2"), 1)
                    wait_freed(act, s, p)
                    A(rs, rs, ACT.Sqrt).then_inc(done("rs"), 1)
                elif s == "zw":
                    wait_filled(act, s, p)
                    A(tw, bank(s)[:, 0:T], ACT.Tanh, bias=dcol(p, 3), scale=0.5).then_inc(free(s), 1)
                elif s == "za":
                    wait_filled(act, s, p)
                    A(ta, bank(s)[:, 0:T], ACT.Tanh, bias=dcol(p, 4), scale=0.5).then_inc(free(s), 1)
                elif s == "gg":
                    wait_filled(act, s, p)
                    wait_done_before(act, "y", p)
                    A(gg, bank(s)[:, 0:T], ACT.Copy).then_inc(free(s), 1)
                elif s == "pe":
                    wait_done(act, "cum", p)
                    A(e1, c1, ACT.Exp)
                    A(e0, c0, ACT.Exp)
                    A(ei, c1, ACT.Exp, scale=-1.0).then_inc(done("exps"), 1)
                elif s in ("tv", "tb", "tk"):
                    wait_filled(act, s, p)
                    A(tok[:, ("tv", "tb", "tk").index(s), :, :], bank(s)[:, :].rearrange("p (c n) -> p c n", c=NC), ACT.Copy).then_inc(free(s), 1)
                elif s == "ts":
                    wait_filled(act, s, p)
                    wait_done_before(act, "vx", p)
                    A(tokS[:, :, :], bank(s)[:, 0:384].rearrange("p (c n) -> p c n", c=3), ACT.Copy).then_inc(free(s), 1)
                elif s[0] == "z":
                    wait_filled(act, s, p)
                    if s[1] == "s":
                        A(Z[:, NC, :], bank(s)[:, 0:P], ACT.Copy).then_inc(free(s), 1)
                    else:
                        A(Z[:, 0:NC, :], bank(s)[:, :].rearrange("p (c n) -> p c n", c=NC), ACT.Copy).then_inc(free(s), 1)
                    if s == "z5":
                        A(wcs, e1[:, 0:TP].rearrange("p (c n) -> p c n", c=NC)[:, :, C - 1:C].rearrange("p c n -> p (c n)"), ACT.Copy)
                elif s in ("s0", "s1", "s2", "s3"):
                    c = int(s[1])
                    wait_filled(act, s, p)
                    if c == 0 and not first(p):
                        act.wait_ge(out_done["S"], 32 * p)
                    A(S, bank(s)[:, 0:P], ACT.Copy, scale=wc(c)).then_inc(free(s), 1)
                elif s == "rs0":
                    wait_filled(act, s, p)
                    A(RTs, bank(s)[:, 0:192], ACT.Copy).then_inc(free(s), 1)
                elif s == "va":
                    wait_filled(act, s, p)
                    A(yq, bank(s)[:, 0:T], ACT.Sqrt, bias=eps[:, 1:2], scale=1.0 / HD).then_inc(free(s), 1)
                elif s == "ms":
                    wait_filled(act, s, p)
                    A(rtmp, bank(s)[:, 0:T], ACT.Sqrt, bias=eps[:, 0:1], scale=1.0 / P).then_inc(free(s), 1)
                elif s == "mu":
                    wait_done(act, "ydev", p)
                    A(yq, y, ACT.Square).then_inc(done("ysq"), 1)
                elif s == "tkk":
                    wait_filled(act, s, p)
                    act.wait_ge(hc_in, 16 * (p + 1))
                    A(kdt[:, 0:2 * P], bank(s)[:, 0:2 * P], ACT.Copy, scale=hcol[:, 0:1])
                    A(kdt[0:HD, 2 * P:3 * P], bank(s)[0:HD, 2 * P:3 * P], ACT.Copy, scale=hcol[0:HD, 1:2]).then_inc(free(s), 1)
                elif s == "tvv":
                    wait_filled(act, s, p)
                    wait_done_before(act, "vrx", p)
                    A(vrt[:, 0:2 * P], bank(s)[:, 0:2 * P], ACT.Copy)
                    A(vrt[0:HD, 2 * P:3 * P], bank(s)[0:HD, 2 * P:3 * P], ACT.Copy).then_inc(free(s), 1)
                    wait_done_before(act, "ret", p)
                    A(gt, rr["g"], ACT.Tanh, scale=0.5).then_inc(done("gt"), 1)
                elif s == "rt1":
                    wait_filled(act, s, p)
                    wait_done_before(act, "r2", p)
                    A(R1, bank(s)[:, 0:P], ACT.Copy).then_inc(free(s), 1)
                elif s == "oo":
                    wait_filled(act, s, p)
                    A(rr["q"], bank(s)[:, 0:T], ACT.Copy)
                    A(rr["kr"], bank(s)[:, 0:T], ACT.Square).then_inc(free(s), 1)

            def pair(p, now, late):
                for it in schedule(now, late):
                    if it[0] == "out":
                        proj(p - it[2], it[1])
                    elif it[0] == "step":
                        step(p - it[2], it[1])

            n_setup = n[1]
            pair(0, True, False)
            assert n[1] - n_setup == ACHAIN[0], n[1] - n_setup
            n0 = n[1]
            with act.Fori(1, PAIRS) as p:
                n[0], n[1] = n0 + (p - 1) * sum(ACHAIN), 0
                pair(p, True, True)
                assert n[1] == sum(ACHAIN), n[1]
            n[0], n[1] = n0 + (PAIRS - 1) * sum(ACHAIN), 0
            pair(PAIRS, False, True)
            assert n[1] == ACHAIN[1]
            n[0], n[1] = n0 + (PAIRS - 1) * sum(ACHAIN) + ACHAIN[1], 0

            for g in range(4):
                act.wait_ge(tr_full, g + 1)
                for t, (t0, nt) in enumerate(TT_):
                    last = A(x1[0:nt, t, g * F:(g + 1) * F], OB[t][0:nt, :], ACT.Copy)
                last.then_inc(tr_free, 1)
            use = Use()
            act.wait_ge(named["ss_zero"], 1)
            for t, (t0, nt) in enumerate(TT_):
                A(yp[0:nt, :], x1[0:nt, t, :], ACT.Square, accum_out=ss[0:nt, t:t + 1])
            A(rstd, ss, ACT.Sqrt, bias=eps[:, 0:1], scale=1.0 / D).then_inc(named["root_done"], 1)
            act.wait_ge(named["cmax_done"], 1)
            A(q4[:, :, :], q4[:, :, :], ACT.Exp).then_inc(named["cexp_done"], 1)
            act.wait_ge(named["dm_done"], 1)
            A(e2, e2, ACT.Exp).then_inc(named["e2_done"], 1)

            def arrived():
                b, k = use.next()
                act.wait_ge(x_full[b], k + 1)
                return b

            def experts(it, more, before, again):
                if again:
                    act.wait_ge(named["h_done"], it)
                act.wait_ge(ex_used, 24 * it + 16)
                A(th, GB[:, :], ACT.Tanh, scale=0.5).then_inc(named["tanh_done"], 1)
                use.k += 4 * more
                b = arrived()
                A(hhT[:, :, :], XB[b][:, :].rearrange("p (k n) -> p k n", k=4), ACT.Copy).then_inc(named["hhT_done"], 1).then_inc(x_free[b], 1)
                use.k += 12 * before
                b = arrived()
                A(gT, XB[b][:, 0:T], ACT.Copy).then_inc(named["gT_done"], 1).then_inc(x_free[b], 1)
                act.wait_ge(ex_used, 24 * it + 24)
                for m in range(NB):
                    last = A(yp[:, m * F:(m + 1) * F], DB[m][:, :], ACT.Copy)
                last.then_inc(named["d_free"], 1)

            def round_of_experts(rd, at_op):
                half, at = EP * XUSES // 2 * rd, EP * rd
                n[0], n[1] = at_op, 0
                use.base(half)
                use.k += 4
                experts(at, True, False, not first(rd))
                each = n[1]
                with act.Fori(1, EP - 1) as i:
                    n[0], n[1] = at_op + each * i, 0
                    use.base(half + XUSES // 2 * i - 4)
                    experts(at + i, True, True, True)
                n[0], n[1] = at_op + each * (EP - 1), 0
                use.base(half + XUSES // 2 * (EP - 1) - 4)
                experts(at + EP - 1, False, True, True)
                return each * EP

            act.wait_ge(named["routed"], 1)
            r = act.value_load(nround[0:1, 0:1], min_val=1, max_val=ROUNDS)
            base = n[0] + n[1]
            per = round_of_experts(0, base)
            with act.If(r > 1):
                with act.Fori(1, r) as rd:
                    round_of_experts(rd, base + per * rd)
                act.nop()
            with act.Else():
                act.nop()
            n[0], n[1] = base + per * r, 0
            act.wait_ge(named["acc_done"], 1)
            for t, (t0, nt) in enumerate(TT_):
                A(yp[0:nt, :], acc[0:nt, t, :], ACT.Square, accum_out=ss[0:nt, t:t + 1])
            A(rstd, ss, ACT.Sqrt, bias=eps[:, 0:1], scale=1.0 / D).then_inc(named["fin_root"], 1)

        @block.vector
        def _(dve):
            v = nc.vector
            n = [0, 0]

            def chained(build):
                def op(*args):
                    ins = build(*args)
                    n[1] += 1
                    ins.then_inc(vchain, 1)
                    dve.wait_ge(vchain, n[0] + n[1])
                    return Over(dve)
                return op

            TT, TSC, STT, CP = (chained(f) for f in (v.tensor_tensor, v.tensor_scalar, v.scalar_tensor_tensor, v.tensor_copy))
            SCAN, RECIP, FILL, RED = (chained(f) for f in (v.tensor_tensor_scan, v.reciprocal, v.memset, v.tensor_reduce))

            FILL(eps[:, 0:1], NORM_EPS)
            FILL(eps[:, 1:2], LNX_EPS)
            FILL(ones, 1.0).then_inc(sem("ones_set"), 1)
            for r_ in ("r", "k", "v"):
                FILL(raw[r_][:, 0:1], 0.0)
            FILL(sh_out, 0.0)
            FILL(AR, 0.0)
            FILL(Bd, 0.0)
            FILL(Kd_, 0.0)
            FILL(Vd, 0.0)
            FILL(S0, 0.0).then_inc(zeroed, 1)
            dve.wait_ge(sem("gain_in"), 16)
            dve.wait_ge(sem("rms_root"), 1)
            RECIP(bsv, bsv)
            for kt in range(KT):
                STT(hT[:, kt, :], hT[:, kt, :], gm[:, kt:kt + 1], bsv, ALU.mult, ALU.mult).then_inc(hT_done, 1)
            dve.wait_ge(const_in, 16 * 4)
            for i in range(3):
                TSC(der[:, :, i:i + 1], prm[:, :, i:i + 1], -1.0, 1.0, ALU.mult, ALU.add)
            for i in range(2):
                TSC(der[:, :, 3 + i:4 + i], prm[:, :, 3 + i:4 + i], 0.5, None, ALU.mult)
            TSC(lmu[:, 3:6], lmu[:, 0:3], -1.0, 1.0, ALU.mult, ALU.add)
            i = PRM.index("k_a")
            TSC(der[:, :, 5:6], prm[:, :, i:i + 1], -0.5, 1.0, ALU.mult, ALU.add)
            TSC(der[:, :, 6:7], prm[:, :, i:i + 1], 0.5, None, ALU.mult)

            def shifted(src, out, mu, one_mu, m, so, written):
                d = src[0:m, 1 + TP:RW].rearrange("p (s n) -> p s n", s=NS)
                dm = mmb[0:m, 1 + TP:RW].rearrange("p (s n) -> p s n", s=NS)
                TSC(mmb[0:m, :], src[0:m, :], mu, None, ALU.mult)
                CP(so[:, 0:1], src[0:m, TP:TP + 1])
                CP(so[:, 1:1 + NS], d[:, :, TS:TS + 1].rearrange("p s n -> p (s n)"))
                STT(out[0:m, 0:TP], src[0:m, 1:1 + TP], one_mu, mmb[0:m, 0:TP], ALU.mult, ALU.add)
                STT(out[0:m, TP:T].rearrange("p (s n) -> p s n", s=NS), d[:, :, 1:1 + TS], one_mu, dm[:, :, 0:TS],
                    ALU.mult, ALU.add).then_inc(written, 1)

            for j, r_ in enumerate("rkv"):
                m = P if j < 2 else 32
                dve.wait_ge(proj_free, j + 1)
                shifted(raw[r_], xm[r_], lmu[0:m, j:j + 1], lmu[0:m, 3 + j:4 + j], m, sh_out[0:m, 24 + j, :], lora_xm)
            dve.wait_ge(sem("lora_tanh"), 1)
            TSC(lg1, lg1, 0.5, 0.5, ALU.mult, ALU.add)
            TSC(lg2[0:32, :], lg2[0:32, :], 0.5, 0.5, ALU.mult, ALU.add).then_inc(lora_done, 1)

            def proj(p, name):
                j = N_TILE[name]
                if j >= 3:
                    return
                dve.wait_ge(proj_free, tile_no(p, j) + 1)
                if name == "v":
                    wait_done_before(dve, "vbd", p)
                if name == "k":
                    wait_done_before(dve, "kk2", p)
                shifted(raw[name], xm[name], scol(p, "mu_" + name), dcol(p, "rkv".index(name)), P, sh_out[:, 8 * "rkv".index(name) + p, :], xms)

            def by_heads(out, op):
                for h in range(2):
                    last = op(out[halves[h], :, h * HD:(h + 1) * HD], halves[h])
                return last

            def step(p, s):
                if s == "ss":
                    wait_filled(dve, s, p)
                    TSC(rs, bank(s)[:, 0:T], 1e-24, None, ALU.max).then_inc(free(s), 1)
                elif s == "pc":
                    wait_freed(dve, "zw", p)
                    TSC(t1, tw, -0.5 * DECAY, -0.5 * DECAY, ALU.mult, ALU.add)
                    SCAN(c1, scanm, t1, 0.0, ALU.mult, ALU.add)
                    TT(c0, c1, t1, ALU.subtract).then_inc(done("cum"), 1)
                elif s == "pa":
                    wait_freed(dve, "za", p)
                    TSC(t2, ta, dcol(p, 6), dcol(p, 5), ALU.mult, ALU.add)
                    TT(kp, xm["k"], t2, ALU.mult)
                    STT(tw, xm["r"], scol(p, "r_k"), kp, ALU.mult, ALU.mult).then_inc(done("bsrc"), 1)
                elif s == "ps":
                    wait_done(dve, "rs", p)
                    RECIP(rs, rs)
                    STT(kn, xm["k"], scol(p, "k_k"), rs, ALU.mult, ALU.mult)
                    STT(t1, ta, 1.0, kn, ALU.add, ALU.mult)
                elif s == "pb":
                    wait_done(dve, "exps", p)
                    if not first(p):
                        dve.wait_ge(full("y"), p)
                    by_heads(AR, lambda o, h: STT(o, heads(kn)[h], -1.0, heads(e0)[h], ALU.mult, ALU.mult))
                    TT(AR[:, :, P:192], heads(xm["r"]), heads(e1), ALU.mult)
                    by_heads(Bd, lambda o, h: STT(o, heads(t1)[h], 0.5, heads(ei)[h], ALU.mult, ALU.mult))
                    by_heads(Kd_, lambda o, h: TT(o, heads(kp)[h], heads(ei)[h], ALU.mult)).then_inc(done("bd"), 1)
                elif s == "bs":
                    wait_filled(dve, s, p)
                    TT(bsv, bank(s)[:, 0:T], xm["v"], ALU.mult).then_inc(free(s), 1)
                elif s in ("g0", "g1", "g2", "g3", "g4"):
                    c = int(s[1])
                    wait_filled(dve, s, p)
                    msk = gmask[c == NC][:, None, :].broadcast_to([P, 2, 192])
                    TT(GM[:, c, :].rearrange("p (a n) -> p a n", a=2), bank(s)[:, 0:384].rearrange("p (a n) -> p a n", a=2), msk, ALU.mult).then_inc(free(s), 1)
                elif s == "lp":
                    wait_filled(dve, s, p)
                    if not first(p):
                        dve.wait_ge(lmk, 5 * p)
                    TT(L[:, 0:NC, :], bank(s)[:, :].rearrange("p (c n) -> p c n", c=NC), lmask[0][:, None, :].broadcast_to([P, NC, P]), ALU.mult).then_inc(free(s), 1)
                elif s == "ls":
                    wait_filled(dve, s, p)
                    TT(L[:, NC, :], bank(s)[:, 0:P], lmask[1], ALU.mult).then_inc(free(s), 1)
                    wait_freed(dve, "g4", p)
                    TT(V[:, :, :], GM[:, :, 0:P], m0T[:, None, :].broadcast_to([P, NCH, P]), ALU.mult)
                    TT(V[:, :, :], V[:, :, :], ident[:, None, :].broadcast_to([P, NCH, P]), ALU.add).then_inc(done("inv0v"), 1)
                elif s[0:2] == "ds":
                    wait_filled(dve, s, p)
                    if s == "ds1":
                        TT(U[:, NC, :], U[:, NC, :], bank(s)[:, P:2 * P], ALU.add)
                    TT(V[:, NC, :], V[:, NC, :], bank(s)[:, 0:P], ALU.add).then_inc(free(s), 1)
                elif s[0] == "d":
                    k = s[1]
                    for x, nm in ((V, "dv"), (U, "du")):
                        if nm + k in bank_of:
                            wait_filled(dve, nm + k, p)
                            if nm + k == "du1":
                                wait_done(dve, "inv0u", p)
                            TT(x[:, 0:NC, :], x[:, 0:NC, :], bank(nm + k)[:, :].rearrange("p (c n) -> p c n", c=NC), ALU.add).then_inc(free(nm + k), 1)
                elif s in ("r0", "r1", "r2", "r3"):
                    wait_filled(dve, s, p)
                    CP(RH, bank(s)[:, 0:P]).then_inc(free(s), 1)
                elif s in ("a0", "a1", "a2", "a3"):
                    wait_filled(dve, s, p)
                    CP(SA, bank(s)[:, 0:P]).then_inc(free(s), 1)
                elif s == "rs1":
                    wait_filled(dve, s, p)
                    CP(RHs, bank(s)[:, 0:P]).then_inc(free(s), 1)
                elif s == "as":
                    wait_filled(dve, s, p)
                    CP(SAs, bank(s)[:, 0:P]).then_inc(free(s), 1)
                    wait_freed(dve, s, p)
                    for h in range(2):
                        last = TT(SAx[halves[h], :, :], SAs[halves[h], None, h * HD:(h + 1) * HD].broadcast_to([HD, NS, HD]),
                                  seqm[halves[h], :, None].broadcast_to([HD, NS, HD]), ALU.mult)
                    last.then_inc(done("sax"), 1)
                elif s == "us":
                    wait_filled(dve, s, p)
                    if not first(p):
                        dve.wait_ge(out_done["So"], 16 * p)
                    pb = bank(s)[:, :].rearrange("p (s n) -> p s n", s=NS)
                    TT(So[halves[0], :, :], S0[halves[0], :, 0:HD], pb[halves[0], :, :], ALU.add)
                    TT(So[halves[1], :, :], S0[halves[1], :, HD:P], pb[halves[1], :, :], ALU.add)
                    w = e1[:, TP:T].rearrange("p (s n) -> p s n", s=NS)[:, :, TS - 1:TS].broadcast_to([P, NS, HD])
                    TT(So[:, :, :], So[:, :, :], w, ALU.mult).then_inc(free(s), 1)
                    dve.wait_ge(free(s), nth(s, p))
                    dve.nop().then_inc(done("so"), 1)
                elif s == "mu":
                    wait_filled(dve, "y", p)
                    CP(y[:, 0:TP], psum["YB"][:, 0:TP])
                    TT(y[:, TP:T], psum["YB"][:, TP:T], RTs[:, P:192], ALU.add).then_inc(free("y"), 1)
                    wait_freed(dve, "y", p)
                    dve.nop().then_inc(done("yin"), 1)
                    wait_filled(dve, s, p)
                    STT(y, bank(s)[:, 0:T], -1.0 / HD, y, ALU.mult, ALU.add).then_inc(free(s), 1)
                    wait_freed(dve, s, p)
                    dve.nop().then_inc(done("ydev"), 1)
                elif s == "pv":
                    wait_freed(dve, "va", p)
                    RECIP(yq, yq)
                    STT(y, y, scol(p, "lnx_g"), yq, ALU.mult, ALU.mult)
                    STT(y, y, scol(p, "lnx_b"), bsv, ALU.add, ALU.add)
                    TT(yT[:, p, :], y, gg, ALU.mult).then_inc(done("y"), 1)
                elif s in ("rq", "rk"):
                    x = rr["q" if s == "rq" else "kr"]
                    wait_filled(dve, s, p)
                    TT(rtmp, bank(s)[:, 0:T], sin, ALU.mult).then_inc(free(s), 1)
                    TT(x, x, cos, ALU.mult)
                    if s == "rq":
                        TT(x, x, rtmp, ALU.add)
                        dve.wait_ge(hc_in, 16 * (p + 1))
                        TT(qd, x, dq, ALU.mult).then_inc(done("qrot"), 1)
                    else:
                        TT(x, x, rtmp, ALU.add).then_inc(done("krot"), 1)
                elif s == "sc":
                    wait_filled(dve, s, p)
                    TT(st[:, 0:TP].rearrange("p (c n) -> p c n", c=2), bank(s)[:, 0:TP].rearrange("p (c n) -> p c n", c=2),
                       maskP[:, None, :].broadcast_to([P, 2, P]), ALU.mult)
                    TT(st[0:HD, TP:T], bank(s)[0:HD, TP:T], maskS[0:HD, 0:HD], ALU.mult).then_inc(free(s), 1)
                elif s == "rt2":
                    wait_filled(dve, s, p)
                    if not first(p):
                        dve.wait_ge(out_done["R2"], 16 * p)
                    STT(R2, R1, hcol[:, 2:3], bank(s)[:, 0:P], ALU.mult, ALU.add).then_inc(free(s), 1)
                    wait_freed(dve, s, p)
                    dve.nop().then_inc(done("r2"), 1)
                elif s == "ms":
                    wait_freed(dve, s, p)
                    RECIP(rtmp, rtmp)
                    wait_done(dve, "gt", p)
                    STT(gt, gt, 1.0, rr["g"], ALU.add, ALU.mult)
                    TT(gt, gt, rr["q"], ALU.mult)
                    STT(yT[:, p + PAIRS, :], gt, 0.5, rtmp, ALU.mult, ALU.mult).then_inc(done("ret"), 1)
                elif s in ("u1", "u2"):
                    i = int(s[1]) - 1
                    wait_filled(dve, s, p)
                    x = Rs0[:, 4 * i:4 * i + 4, :]
                    STT(x, x, hcol[:, 3:4], bank(s)[:, :].rearrange("p (s n) -> p s n", s=4), ALU.mult, ALU.add).then_inc(free(s), 1)
                    if s == "u2":
                        wait_freed(dve, s, p)
                        dve.nop().then_inc(done("u"), 1)

            def pair(p, now, late):
                for it in schedule(now, late):
                    if it[0] == "out":
                        proj(p - it[2], it[1])
                    elif it[0] == "step":
                        step(p - it[2], it[1])

            n_setup = n[1]
            pair(0, True, False)
            assert n[1] - n_setup == VCHAIN[0], n[1] - n_setup
            n0 = n[1]
            with dve.Fori(1, PAIRS) as p:
                n[0], n[1] = n0 + (p - 1) * sum(VCHAIN), 0
                pair(p, True, True)
                assert n[1] == sum(VCHAIN), n[1]
            n[0], n[1] = n0 + (PAIRS - 1) * sum(VCHAIN), 0
            pair(PAIRS, False, True)
            assert n[1] == VCHAIN[1], n[1]
            n[0], n[1] = n0 + (PAIRS - 1) * sum(VCHAIN) + VCHAIN[1], 0

            for m in range(KT):
                dve.wait_ge(x_in[m // 4], 16)
                dve.wait_ge(wo_used, m + 1)
                TT(x1T[:, m, :], x1T[:, m, :], psum["PJ%d" % (m % 2)][:, 0:T], ALU.add).then_inc(x1T_done, 1)
                if m == 4:
                    FILL(ss, 0.0).then_inc(named["ss_zero"], 1)
                    FILL(lg, 0.0)
                    dve.wait_ge(r_in, 48)
                    TT(rg[:, :, :], rg[:, :, :], gf[:, :, None].broadcast_to([P, KT, 36]), ALU.mult).then_inc(named["rg_done"], 1)
            dve.wait_ge(named["root_done"], 1)
            RECIP(rstd, rstd)
            dve.wait_ge(named["lgT_full"], 1)
            CP(gT[0:36, :], UB[0:36, 0:T]).then_inc(named["lgT_out"], 1)
            dve.wait_ge(named["lg_full"], 1)
            for t, (t0, nt) in enumerate(TT_):
                TSC(lg[0:nt, t, :], GB[0:nt, t * 64:t * 64 + 36], rstd[0:nt, t:t + 1], None, ALU.mult)

            def wide(x, k):
                return x[:, :, None].broadcast_to([P, 3, k])

            def pick(out, x, top, k, tmp):
                TT(tmp[:, :, :], x, wide(top, k), ALU.is_equal)
                TT(tmp[:, :, :], tmp[:, :, :], iodesc[:, None, EG - k:EG].broadcast_to([P, 3, k]), ALU.mult)
                RED(cm, tmp[:, :, :], AX_X, ALU.max)
                TT(out[:, :, :], tmp[:, :, :], wide(cm, k), ALU.is_equal)

            coarse = lg[:, :, 0:NG]
            RED(m1, coarse, AX_X, ALU.max)
            TT(q4[:, :, :], coarse, wide(m1, NG), ALU.subtract).then_inc(named["cmax_done"], 1)
            pick(goh, coarse, m1, NG, fine4)
            TT(goh[:, :, :], goh[:, :, :], wide(valid, NG), ALU.mult)
            for gi in range(NG):
                src = lg[:, :, NG + gi * EG:NG + (gi + 1) * EG]
                g1 = goh[:, :, gi:gi + 1].broadcast_to([P, 3, EG])
                if gi == 0:
                    TT(lf[:, :, :], src, g1, ALU.mult)
                else:
                    TT(q8[:, :, :], src, g1, ALU.mult)
                    TT(lf[:, :, :], lf[:, :, :], q8[:, :, :], ALU.add)
            RED(m1, lf[:, :, :], AX_X, ALU.max)
            pick(oh1, lf[:, :, :], m1, EG, q8)
            STT(lf2[:, :, :], oh1[:, :, :], -BIG, lf[:, :, :], ALU.mult, ALU.add)
            RED(m2, lf2[:, :, :], AX_X, ALU.max)
            pick(oh2, lf2[:, :, :], m2, EG, q8)
            TT(e2, m2, m1, ALU.subtract).then_inc(named["dm_done"], 1)
            dve.wait_ge(named["cexp_done"], 1)
            RED(csum, q4[:, :, :], AX_X, ALU.add)
            RECIP(pg, csum)
            dve.wait_ge(named["e2_done"], 1)
            TSC(ga, e2, 1.0, None, ALU.add)
            RECIP(ga, ga)
            TT(ga, ga, pg, ALU.mult)
            TT(gb, ga, e2, ALU.mult)
            TT(lf[:, :, :], oh1[:, :, :], wide(ga, EG), ALU.mult)
            TT(q8[:, :, :], oh2[:, :, :], wide(gb, EG), ALU.mult)
            TT(lf[:, :, :], lf[:, :, :], q8[:, :, :], ALU.add)
            TT(oh1[:, :, :], oh1[:, :, :], oh2[:, :, :], ALU.add)
            for gi in range(NG):
                g1 = goh[:, :, gi:gi + 1].broadcast_to([P, 3, EG])
                TT(asg[:, :, gi * EG:(gi + 1) * EG], oh1[:, :, :], g1, ALU.mult)
            last = [TT(gate[:, :, gi * EG:(gi + 1) * EG], lf[:, :, :], goh[:, :, gi:gi + 1].broadcast_to([P, 3, EG]), ALU.mult)
                    for gi in range(NG)]
            last[-1].then_inc(named["asg_done"], 1)
            dve.wait_ge(named["rank_full"], 1)
            STT(sc[:, :, :], UB[:, 0:3 * NE].rearrange("p (t n) -> p t n", t=3), 1.0, asg[:, :, :], ALU.add, ALU.mult)
            TSC(sc[:, :, :], sc[:, :, :], -1.0, None, ALU.add)
            RED(cmx, UB[:, 3 * NE:4 * NE], AX_X, ALU.max)
            TT(over, cmx.broadcast_to([P, ROUNDS - 1]), caps, ALU.is_gt)
            RED(cmx, over, AX_X, ALU.add)
            TSC(nround[:, :], cmx, 1.0, None, ALU.add).then_inc(named["routed"], 1)

            use = Use()
            def arrived():
                b, k = use.next()
                dve.wait_ge(x_full[b], k + 1)
                return b

            def picked(out, i):
                o4 = out[:, :, :].rearrange("p t (e n) -> p t e n", e=2)
                TT(o4, sc[:, :, bass.ds(2 * i, 2)][:, :, :, None].broadcast_to([P, 3, 2, CAP]),
                   slot_no[:, None, None, :].broadcast_to([P, 3, 2, CAP]), ALU.is_equal)
                return o4

            def select(i, it):
                picked(sel, i)
                TT(sel[:, :, :], sel[:, :, :], wide(rstd, P), ALU.mult).then_inc(named["sel_done"], 1)

            def gathered(it):
                for k4 in range(4):
                    b = arrived()
                    last = TT(xg[:, 4 * k4:4 * k4 + 4, :], XB[b][:, :].rearrange("p (k n) -> p k n", k=4),
                              gf[:, 4 * k4:4 * k4 + 4, None].broadcast_to([P, 4, P]), ALU.mult).then_inc(x_free[b], 1)
                last.then_inc(named["xg_done"], 1)

            def combined():
                for t, (t0, nt) in enumerate(TT_):
                    for m in range(NB):
                        b = arrived()
                        a_ = acc[0:nt, t, m * F:(m + 1) * F]
                        TT(a_, a_, XB[b][0:nt, :], ALU.add).then_inc(x_free[b], 1)

            def experts(i, it, more, before, again):
                if again:
                    dve.wait_ge(named["gT_done"], it)
                o4 = picked(selg, i)
                TT(o4, o4, gate[:, :, bass.ds(2 * i, 2)][:, :, :, None].broadcast_to([P, 3, 2, CAP]), ALU.mult).then_inc(named["selg_done"], 1)
                if more:
                    select(i + 1, it + 1)
                dve.wait_ge(named["tanh_done"], it + 1)
                if again:
                    dve.wait_ge(named["hhT_done"], it)
                TSC(th, th, 0.5, 0.5, ALU.mult, ALU.add)
                TT(th, th, GB[:, :], ALU.mult)
                TT(hh, th, UB[:, :], ALU.mult).then_inc(named["h_done"], 1).then_inc(named["gu_free"], 1)
                if more:
                    gathered(it + 1)
                use.k += 1
                if before:
                    combined()
                use.k += 1

            def round_of_experts(rd, at_op):
                half, at = EP * XUSES // 2 * rd, EP * rd
                n[0], n[1] = at_op, 0
                use.base(half)
                if not first(rd):
                    TSC(sc[:, :, :], sc[:, :, :], -float(CAP), None, ALU.add)
                select(0, at)
                gathered(at)
                experts(0, at, True, False, not first(rd))
                k0 = n[1]
                dve.wait_ge(named["acc_init"], 1)
                with dve.Fori(1, EP - 1) as i:
                    n[0], n[1] = at_op + k0 + ECHAIN * (i - 1), 0
                    use.base(half + XUSES // 2 * i - 4)
                    experts(i, at + i, True, True, True)
                    assert n[1] == ECHAIN, n[1]
                n[0], n[1] = at_op + k0 + ECHAIN * (EP - 2), 0
                use.base(half + XUSES // 2 * (EP - 1) - 4)
                experts(EP - 1, at + EP - 1, False, True, True)
                combined()
                return k0 + ECHAIN * (EP - 2) + n[1]

            r = dve.value_load(nround[0:1, 0:1], min_val=1, max_val=ROUNDS)
            base = n[0] + n[1]
            once = round_of_experts(0, base)
            again = once + 1
            with dve.If(r > 1):
                with dve.Fori(1, r) as rd:
                    assert round_of_experts(rd, base + once + again * (rd - 1)) == again
                dve.nop()
            with dve.Else():
                dve.nop()
            n[0], n[1] = base + once + again * (r - 1), 0
            dve.nop().then_inc(named["acc_done"], 1)
            dve.wait_ge(named["fin_root"], 1)
            RECIP(rstd, rstd)
            dve.wait_ge(gfin_in, 16)
            for t, (t0, nt) in enumerate(TT_):
                STT(acc[0:nt, t, :], acc[0:nt, t, :], rstd[0:nt, t:t + 1], gfb[0:nt, :], ALU.mult, ALU.mult).then_inc(named["fin_done"], 1)

        @block.gpsimd
        def _(pool):
            n = [0, 0]

            def TT(*args):
                ins = nc.gpsimd.tensor_tensor(*args)
                n[1] += 1
                ins.then_inc(pchain, 1)
                pool.wait_ge(pchain, n[0] + n[1])
                return Over(pool)

            pool.wait_ge(zeroed, 1)
            pool.wait_ge(const_in, 16 * 4)

            def step(p, s):
                if s == "ls":
                    wait_freed(pool, "lp", p)
                    wait_freed(pool, "ls", p)
                    TT(Lm[:, 1, :, :], L[:, :, :], lvl[1][:, None, :].broadcast_to([P, NCH, P]), ALU.mult).then_inc(lmk, 1)
                    TT(U[:, :, :], L[:, :, :], lvl[0][:, None, :].broadcast_to([P, NCH, P]), ALU.mult)
                    TT(U[:, :, :], U[:, :, :], ident[:, None, :].broadcast_to([P, NCH, P]), ALU.add).then_inc(done("inv0u"), 1)
                    TT(Lm[:, 0, :, :], L[:, :, :], lvl[2][:, None, :].broadcast_to([P, NCH, P]), ALU.mult).then_inc(lmk, 1)
                elif s in ("ds1", "ds2", "d3"):
                    k = {"ds1": 3, "ds2": 4, "d3": 5}[s]
                    if k < 5:
                        wait_filled(pool, "zs%d" % (k - 2), p)
                    wait_filled(pool, "z%d" % (k - 2), p)
                    TT(Lm[:, k % 2, 0:NC, :], L[:, 0:NC, :], lvl[k][:, None, :].broadcast_to([P, NC, P]), ALU.mult).then_inc(lmk, 1)
                elif s == "ts":
                    wait_freed(pool, s, p)
                    wait_before_us(pool, p)
                    for h in range(2):
                        last = TT(Vx[halves[h], :, :], tokS[halves[h], 0, None, h * HD:(h + 1) * HD].broadcast_to([HD, NS, HD]),
                                               seqm[halves[h], :, None].broadcast_to([HD, NS, HD]), ALU.mult)
                    last.then_inc(done("vx"), 1)
                elif s == "tvv":
                    wait_freed(pool, s, p)
                    TT(Vrx[0:HD, :, :], vrt[0:HD, None, 2 * P:3 * P].broadcast_to([HD, NS, P]),
                                    seqm[0:HD, :, None].broadcast_to([HD, NS, P]), ALU.mult).then_inc(done("vrx"), 1)

            def wait_before_us(e, p):
                if not first(p):
                    wait_filled(e, "us", p - 1)

            def pair(p, now, late):
                for it in schedule(now, late):
                    if it[0] == "step":
                        step(p - it[2], it[1])

            pair(0, True, False)
            assert n[1] == PCHAIN[0], n[1]
            with pool.Fori(1, PAIRS) as p:
                n[0], n[1] = PCHAIN[0] + (p - 1) * sum(PCHAIN), 0
                pair(p, True, True)
                assert n[1] == sum(PCHAIN), n[1]
            n[0], n[1] = PCHAIN[0] + (PAIRS - 1) * sum(PCHAIN), 0
            pair(PAIRS, False, True)
            pool.wait_ge(xms, 3 * PAIRS)
            pool.wait_ge(lora_xm, 3)
            pool.dma_start(o_shift, sh_out[:, :, :]).then_inc(out_done["shift"], 16)
            pool.wait_ge(tr_free, 4)
            pool.wait_ge(named["lg_full"], 1)
            for t, (t0, nt) in enumerate(TT_):
                last = nc.gpsimd.tensor_copy(acc[0:nt, t, :], x1[0:nt, t, :])
            last.then_inc(named["acc_init"], 1)


def constants():
    import numpy as np
    f = np.float32
    i = np.arange(P)
    hd, t = i // HD, i % HD
    same = hd[:, None] == hd[None, :]
    rot = np.zeros((P, P), f)
    rot[i[1::2], i[0::2]] = -1.0
    rot[i[0::2], i[1::2]] = 1.0

    def gram(seq):
        ok = (t[:, None] // seq) == (t[None, :] // seq)
        a = same & ok & (t[:, None] < t[None, :])
        tt = np.arange(HD)
        b = (t[:, None] <= tt[None, :]) & ((t[:, None] // seq) == (tt[None, :] // seq))
        return np.concatenate([a, b], 1).astype(f), a.T.astype(f)

    (g0, l0), (g1, l1) = gram(C), gram(TS)

    def level(k):
        b = 1 << k
        return (same & ((t[:, None] // (2 * b)) == (t[None, :] // (2 * b)))
                & ((t[:, None] // b) % 2 == 1) & ((t[None, :] // b) % 2 == 0)).astype(f)

    lv = [level(k) for k in range(LEVELS)]
    tri = (i[:, None] < i[None, :]).astype(f)
    tok = np.arange(T)
    start = np.where(tok < TP, tok % C == 0, (tok - TP) % TS == 0)
    scan = np.broadcast_to(1.0 - start.astype(f), (P, T))
    pos = np.where(tok < TP, tok, PAST_LEN + (tok - TP) % TS).astype(f)
    theta = (f(1.0) / (f(10000.0) ** np.linspace(0.0, 1.0, HD, dtype=f))).astype(f)
    ang = (pos[None, :] * np.repeat(theta, 2)[:, None]).astype(f)
    cos, sin = np.cos(ang).astype(f), np.sin(ang).astype(f)
    seqm = ((t[:, None] // TS) == np.arange(NS)[None, :]).astype(f)
    cst = np.concatenate([np.eye(P), same, rot, lv[0].T, g0, g1, l0, l1, *lv, tri, scan, cos, sin, seqm], 1)
    lg = np.log1p(-(2.0 ** (-5.0 - np.arange(PAIRS))))
    head = np.zeros((PAIRS, P, HC), f)
    for h in range(PAIRS):
        dif = i[None, :] - i[:, None]
        head[h, :, 0:P] = np.where(dif >= 0, np.exp(np.maximum(dif, 0) * lg[h]), 0.0)
        ok = (dif >= 0) & (i[None, :] // TS == i[:, None] // TS)
        head[h, :, P:2 * P] = np.where(ok, np.exp(np.maximum(dif, 0) * lg[h]), 0.0)
        at = np.where(tok < TP, tok % P, (tok - TP) % TS)
        head[h, :, 2 * P:2 * P + T] = np.exp((at + 1.0) * lg[h])[None, :]
        head[h, :, 2 * P + T] = np.exp((P - 1.0 - i) * lg[h])
        head[h, :, 2 * P + T + 1] = np.exp((TS - 1.0 - i % TS) * lg[h])
        head[h, :, 2 * P + T + 2] = np.exp(P * lg[h])
        head[h, :, 2 * P + T + 3] = np.exp(TS * lg[h])
    return np.ascontiguousarray(cst.astype(f)), head


def kernel(**inp):
    import numpy as np
    import concourse.bacc as bacc
    from concourse.bass_utils import run_bass_kernel_spmd

    a = {k: np.asarray(v) for k, v in inp.items()}
    x = np.concatenate([a["x_prompt"].reshape(TP, D), a["x_sample"].reshape(NS * TS, D)], 0)
    w = a["w_in"][0]
    A = PAIRS * P
    lo = 3 * A
    w3 = w[:, lo:lo + 288]
    ret = w[:, lo + 288:]
    rt = ret.reshape(D, 4, PAIRS, P)
    rk = w[:, :lo].reshape(D, 3, PAIRS, P)[:, [1, 0, 2]]
    pairs = np.concatenate([rk, rt], 1).transpose(2, 1, 0, 3).reshape(7 * PAIRS, D, P)
    low = np.concatenate([w3, np.zeros((D, 3 * P - 288), np.float32)], 1).reshape(D, 3, P).transpose(1, 0, 2)
    win = np.concatenate([low, pairs], 0).reshape(NTILE, KT, P, P).transpose(0, 2, 1, 3).reshape(NTILE, P, KT * P)

    def chan(v):
        return v.reshape(PAIRS, P).T

    mu = a["mu_shift"][0]
    params = np.stack([chan(mu[0:A]), chan(mu[A:2 * A]), chan(mu[2 * A:lo]), chan(a["decay_w0"][0]), chan(a["iclr_a0"][0]),
                       chan(a["k_k"][0]), chan(a["k_a"][0]), chan(a["r_k"][0].reshape(-1)), chan(a["lnx_g"][0]),
                       chan(a["lnx_b"][0])], 2)

    def pad288(v):
        return np.concatenate([v, np.zeros(v.shape[:-1] + (3 * P - 288,), np.float32)], -1).reshape(v.shape[:-1] + (3, P))

    lora_mu = pad288(mu[lo:]).T
    sh = a["state_rwkv_shift"][0]
    shT = np.concatenate([sh[:, :lo].reshape(NS, 24, P), pad288(sh[:, lo:])], 1).transpose(2, 1, 0)
    gu = a["gate_up"][0]
    gu2 = np.concatenate([gu[P:], np.zeros((2 * P - 160, A), np.float32)], 0)
    lora_w = np.stack([np.concatenate([a["decay_up"][0], a["iclr_up"][0]], 0), gu[:P], gu2], 1)
    lora_w = lora_w.reshape(P, 3, PAIRS, P).transpose(2, 0, 1, 3).reshape(PAIRS, P, 3 * P)
    s0 = a["state_rwkv_wkv"][0].reshape(NS, PAIRS, 2, HD, HD).transpose(1, 2, 4, 0, 3)
    r0 = a["state_retention"][0].transpose(1, 2, 0, 3)
    cst, head = constants()
    rcst = np.ones((P, EG + CAP + 3 + ROUNDS - 1), np.float32)
    rcst[:, :EG] = EG - np.arange(EG)
    rcst[:, EG:EG + CAP] = np.arange(CAP)
    rcst[NS * TS:, EG + CAP + 2] = 0.0
    rcst[:, EG + CAP + 3:] = CAP * np.arange(1, ROUNDS)
    c = np.ascontiguousarray
    ins = {
        "xT": c(x.T.reshape(KT, P, T).transpose(1, 0, 2)), "win": c(win),
        "w_out": c(a["w_out"][0].reshape(KT, P, KT, P)[KORD].transpose(2, 1, 0, 3).reshape(KT, P, KT * P)),
        "params": c(params), "lora_mu": c(lora_mu), "shT": c(shT), "lora_w": c(lora_w),
        "router": c(np.concatenate([a["router_coarse"][0], a["router_fine"][0].transpose(1, 0, 2).reshape(D, NE)], 1)
                    .reshape(KT, P, NG + NE).transpose(1, 0, 2)),
        "gffn": c(a["norm_ffn_g"][0].reshape(KT, P).T), "gfin": c(np.broadcast_to(a["norm_final_g"], (P, D))),
        "rcst": rcst, "w_gate": a["exp_w_gate"][0], "w_up": a["exp_w_up"][0], "w_down": a["exp_w_down"][0],
        "gmix": c(a["norm_mix_g"][0].reshape(KT, P).T), "cst": cst, "head_cst": head, "s0_wkv": c(s0), "s0_ret": c(r0),
    }
    outs = {"o_y": [T, D], "o_shift": [P, 27, NS + 1], "o_pwkv": [PAIRS, 2, HD, HD], "o_pret": [PAIRS, P, P],
            "o_swkv": [PAIRS, P, NS, HD], "o_sret": [PAIRS, P, NS, P]}
    nc = bacc.Bacc("TRN2", target_bir_lowering=False, num_devices=1)
    args = {n: nc.dram_tensor(n, list(v.shape), F32, kind="ExternalInput").ap() for n, v in ins.items()}
    args |= {n: nc.dram_tensor(n, s, F32, kind="ExternalOutput").ap() for n, s in outs.items()}
    build_program(nc, **args)
    r = run_bass_kernel_spmd(nc, [ins], core_ids=[0]).results[0]
    o = r["o_y"]
    shift = r["o_shift"].transpose(2, 1, 0).reshape(NS + 1, 27 * P)[:, :lo + 288]
    pw = r["o_pwkv"].transpose(0, 1, 3, 2).reshape(1, 1, 16, HD, HD)
    sw = r["o_swkv"].reshape(PAIRS, 2, HD, NS, HD).transpose(3, 0, 1, 4, 2).reshape(1, NS, 16, HD, HD)
    return (c(o[:TP].reshape(1, TP, D)), c(o[TP:].reshape(NS, TS, D)), c(shift[0:1][None]), c(pw),
            c(r["o_pret"][None, None]), c(shift[1:][None]), c(sw), c(r["o_sret"].transpose(2, 0, 1, 3)[None]))
```
